# Optimizing a Trainium2 kernel written in Bass

```python
import math
import jax, jax.numpy as jnp
from jax import lax
import numpy as np

D_MODEL = 1024
BATCH = 1
SEQ = 1024
DEPTH = 1
DEC_BATCH = 1
DEC_SEQ = 32
PAST_LEN = 128

CHUNK = 64
Q_BLOCK = 128
RET_HEADS = 4
RET_DK = 128
RET_DV = 256
DA_HEADS = 4
DA_DK = 128
DA_DV = 256
D_FF = 2816
CONV_W = 3
PLE_DIM = 256
ROPE_THETA = 10000.0
EPS = 1e-6

RET_QK = RET_HEADS * RET_DK
RET_V = RET_HEADS * RET_DV
DA_QK = DA_HEADS * 2 * DA_DK
DA_V = DA_HEADS * DA_DV
IN_WIDTHS = (RET_QK, RET_QK, RET_V, RET_V, DA_QK, DA_QK, DA_V, D_MODEL, D_MODEL)
D_IN = sum(IN_WIDTHS)
SPLIT_IDX = [int(v) for v in np.cumsum(IN_WIDTHS)[:-1]]

kernel_name = 'hybrid_retention_diffattn_stream_step'

def rms_norm(x, g=None):
    xf = x.astype(jnp.float32)
    y = xf * lax.rsqrt(jnp.mean(xf * xf, axis=-1, keepdims=True) + EPS)
    if g is not None:
        y = y * g.astype(jnp.float32)
    return y.astype(x.dtype)

def rope(x, pos):
    d = x.shape[-1]
    inv = ROPE_THETA ** (-jnp.arange(0, d, 2, dtype=jnp.float32) / d)
    ang = pos.astype(jnp.float32)[:, None] * inv[None, :]
    ang = jnp.concatenate([ang, ang], axis=-1)
    shape = (1, pos.shape[0]) + (1,) * (x.ndim - 3) + (d,)
    cos = jnp.cos(ang).reshape(shape)
    sin = jnp.sin(ang).reshape(shape)
    xf = x.astype(jnp.float32)
    rot = jnp.concatenate([-xf[..., d // 2:], xf[..., :d // 2]], axis=-1)
    return (xf * cos + rot * sin).astype(x.dtype)

def ret_log_gamma():
    return jnp.log(1.0 - jnp.exp2(-5.0 - jnp.arange(RET_HEADS, dtype=jnp.float32)))

def retention_chunk(q, k, v, S, log_g):
    C = q.shape[1]
    idx = jnp.arange(C, dtype=jnp.float32)
    diff = idx[:, None] - idx[None, :]
    decay = jnp.where(diff >= 0, jnp.exp(log_g[:, None, None] * jnp.maximum(diff, 0.0)), 0.0)
    scores = jnp.einsum('bihd,bjhd->bhij', q, k) * decay[None]
    intra = jnp.einsum('bhij,bjhe->bihe', scores, v)
    q_decay = jnp.exp((idx + 1.0)[:, None] * log_g[None, :])
    inter = jnp.einsum('bihd,bhde->bihe', q, S) * q_decay[None, :, :, None]
    k_decay = jnp.exp((C - 1.0 - idx)[:, None] * log_g[None, :])
    S_new = jnp.exp(C * log_g)[None, :, None, None] * S + jnp.einsum('bjhd,bjhe->bhde', k * k_decay[None, :, :, None], v)
    return intra + inter, S_new

def retention_prompt(q, k, v, log_g):
    B, S = q.shape[:2]
    n = S // CHUNK
    def to_chunks(t):
        return t.reshape((B, n, CHUNK) + t.shape[2:]).transpose(1, 0, 2, 3, 4)
    def step(state, xs):
        qc, kc, vc = xs
        o, state = retention_chunk(qc, kc, vc, state, log_g)
        return state, o
    S0 = jnp.zeros((B, RET_HEADS, RET_DK, RET_DV), jnp.float32)
    S_fin, o = lax.scan(step, S0, (to_chunks(q), to_chunks(k), to_chunks(v)))
    o = o.transpose(1, 0, 2, 3, 4).reshape(B, S, RET_HEADS, RET_DV)
    return o, S_fin

def diff_core(q, k, v, mask, lam):
    s = jnp.einsum('bqhmd,bkhmd->bhmqk', q, k, preferred_element_type=jnp.float32) * (DA_DK ** -0.5)
    if mask is not None:
        s = jnp.where(mask, s, jnp.finfo(jnp.float32).min)
    p = jax.nn.softmax(s, axis=-1)
    a = p[:, :, 0] - lam * p[:, :, 1]
    return jnp.einsum('bhqk,bkhe->bqhe', a.astype(v.dtype), v)

def diff_attn_prompt(q, k, v, lam):
    B, S = q.shape[:2]
    nb = S // Q_BLOCK
    qb = q.reshape(B, nb, Q_BLOCK, DA_HEADS, 2, DA_DK).transpose(1, 0, 2, 3, 4, 5)
    k_chunk = jnp.arange(S) // CHUNK
    def one_block(args):
        qi, bi = args
        q_chunk = (bi * Q_BLOCK + jnp.arange(Q_BLOCK)) // CHUNK
        mask = k_chunk[None, :] <= q_chunk[:, None]
        return diff_core(qi, k, v, mask, lam)
    o = lax.map(one_block, (qb, jnp.arange(nb)))
    return o.transpose(1, 0, 2, 3, 4).reshape(B, S, DA_HEADS, DA_DV)

def layer(x, ple, pos, past, lp, layer_idx):
    B, T, _ = x.shape
    h = rms_norm(x, lp['g_mix'])
    z = h @ lp['w_in']
    rq, rk, rv, rg, dq, dk, dv, ga, gb = jnp.split(z, SPLIT_IDX, axis=-1)

    log_g = ret_log_gamma()
    rq = rope(rq.reshape(B, T, RET_HEADS, RET_DK), pos).astype(jnp.float32)
    rk = (rope(rk.reshape(B, T, RET_HEADS, RET_DK), pos) * (RET_DK ** -0.5)).astype(jnp.float32)
    rv = rv.reshape(B, T, RET_HEADS, RET_DV).astype(jnp.float32)
    if past is None:
        o_r, S_new = retention_prompt(rq, rk, rv, log_g)
    else:
        o_r, S_new = retention_chunk(rq, rk, rv, past[2].astype(jnp.float32), log_g)
    o_r = rms_norm(o_r).astype(x.dtype).reshape(B, T, RET_V) * jax.nn.silu(rg)
    branch_a = o_r @ lp['w_ret_br']

    lam_init = 0.8 - 0.6 * math.exp(-0.3 * layer_idx)
    lam = (jnp.exp(jnp.sum(lp['lam_q1'].astype(jnp.float32) * lp['lam_k1'].astype(jnp.float32)))
           - jnp.exp(jnp.sum(lp['lam_q2'].astype(jnp.float32) * lp['lam_k2'].astype(jnp.float32))) + lam_init)
    dq = rope(rms_norm(dq.reshape(B, T, DA_HEADS, 2, DA_DK), lp['g_qn']), pos)
    dk = rope(rms_norm(dk.reshape(B, T, DA_HEADS, 2, DA_DK), lp['g_kn']), pos)
    dv = dv.reshape(B, T, DA_HEADS, DA_DV)
    if past is None:
        o_d = diff_attn_prompt(dq, dk, dv, lam)
    else:
        k_all = jnp.concatenate([past[0].astype(dk.dtype), dk], axis=1)
        v_all = jnp.concatenate([past[1].astype(dv.dtype), dv], axis=1)
        o_d = diff_core(dq, k_all, v_all, None, lam)
    o_d = (rms_norm(o_d, lp['g_dnorm']) * (1.0 - lam_init)).reshape(B, T, DA_V)
    branch_b = o_d @ lp['w_da_br']

    m = jax.nn.sigmoid(ga) * branch_a + jax.nn.sigmoid(gb) * branch_b
    x = x + m @ lp['w_out']

    u = rms_norm(x, lp['g_ffn']) @ lp['w_up']
    buf = jnp.zeros((B, CONV_W - 1, 2 * D_FF), u.dtype) if past is None else past[3].astype(u.dtype)
    u_full = jnp.concatenate([buf, u], axis=1)
    cw = lp['conv_w']
    c = sum(cw[j] * u_full[:, j:j + T] for j in range(CONV_W)) + lp['conv_b']
    cg, cv = jnp.split(c, 2, axis=-1)
    x = x + (jax.nn.silu(cg) * cv) @ lp['w_down']
    conv_new = u_full[:, -(CONV_W - 1):]

    x = x + jax.nn.sigmoid(rms_norm(x, lp['g_ple']) @ lp['w_ple_gate']) * (ple @ lp['w_ple'])
    return x, (dk, dv, S_new, conv_new)

def setup_inputs(seed: int = 0) -> dict:
    key = jax.random.key(seed)
    ks = iter(jax.random.split(key, 32))
    def nrm(shape, scale):
        return jax.random.normal(next(ks), shape, jnp.float32) * scale
    def gain(shape):
        return 1.0 + nrm(shape, 0.02)
    return {
        'x_prompt': nrm((BATCH, SEQ, D_MODEL), 1.0),
        'x_sample': nrm((DEC_BATCH, DEC_SEQ, D_MODEL), 1.0),
        'cache_k': nrm((DEPTH, DEC_BATCH, PAST_LEN, DA_HEADS, 2, DA_DK), 1.0),
        'cache_v': nrm((DEPTH, DEC_BATCH, PAST_LEN, DA_HEADS, DA_DV), 1.0),
        'state_ret': nrm((DEPTH, DEC_BATCH, RET_HEADS, RET_DK, RET_DV), 0.3),
        'state_conv': nrm((DEPTH, DEC_BATCH, CONV_W - 1, 2 * D_FF), 1.0),
        'p_prompt': nrm((DEPTH, BATCH, SEQ, PLE_DIM), 1.0),
        'p_sample': nrm((DEPTH, DEC_BATCH, DEC_SEQ, PLE_DIM), 1.0),
        'g_mix': gain((DEPTH, D_MODEL)),
        'w_in': nrm((DEPTH, D_MODEL, D_IN), D_MODEL ** -0.5),
        'g_qn': gain((DEPTH, DA_DK)),
        'g_kn': gain((DEPTH, DA_DK)),
        'lam_q1': nrm((DEPTH, DA_DK), 0.1),
        'lam_k1': nrm((DEPTH, DA_DK), 0.1),
        'lam_q2': nrm((DEPTH, DA_DK), 0.1),
        'lam_k2': nrm((DEPTH, DA_DK), 0.1),
        'g_dnorm': gain((DEPTH, DA_DV)),
        'w_ret_br': nrm((DEPTH, RET_V, D_MODEL), RET_V ** -0.5),
        'w_da_br': nrm((DEPTH, DA_V, D_MODEL), DA_V ** -0.5),
        'w_out': nrm((DEPTH, D_MODEL, D_MODEL), D_MODEL ** -0.5),
        'g_ffn': gain((DEPTH, D_MODEL)),
        'w_up': nrm((DEPTH, D_MODEL, 2 * D_FF), D_MODEL ** -0.5),
        'conv_w': nrm((DEPTH, CONV_W, 2 * D_FF), CONV_W ** -0.5),
        'conv_b': nrm((DEPTH, 2 * D_FF), 0.02),
        'w_down': nrm((DEPTH, D_FF, D_MODEL), D_FF ** -0.5),
        'g_ple': gain((DEPTH, D_MODEL)),
        'w_ple_gate': nrm((DEPTH, D_MODEL, D_MODEL), D_MODEL ** -0.5),
        'w_ple': nrm((DEPTH, PLE_DIM, D_MODEL), PLE_DIM ** -0.5),
    }

def reference(x_prompt, x_sample, cache_k, cache_v, state_ret, state_conv, p_prompt, p_sample,
              g_mix, w_in, g_qn, g_kn, lam_q1, lam_k1, lam_q2, lam_k2, g_dnorm, w_ret_br, w_da_br,
              w_out, g_ffn, w_up, conv_w, conv_b, w_down, g_ple, w_ple_gate, w_ple):
    pos_p = jnp.arange(x_prompt.shape[1])
    pos_s = PAST_LEN + jnp.arange(x_sample.shape[1])
    yp, ys = x_prompt, x_sample
    kp, ks_, vp, vs, rp, rs, cp, cs = [], [], [], [], [], [], [], []
    for i in range(DEPTH):
        lp = dict(g_mix=g_mix[i], w_in=w_in[i], g_qn=g_qn[i], g_kn=g_kn[i], lam_q1=lam_q1[i],
                  lam_k1=lam_k1[i], lam_q2=lam_q2[i], lam_k2=lam_k2[i], g_dnorm=g_dnorm[i],
                  w_ret_br=w_ret_br[i], w_da_br=w_da_br[i], w_out=w_out[i], g_ffn=g_ffn[i],
                  w_up=w_up[i], conv_w=conv_w[i], conv_b=conv_b[i], w_down=w_down[i],
                  g_ple=g_ple[i], w_ple_gate=w_ple_gate[i], w_ple=w_ple[i])
        yp, (k1, v1, s1, c1) = layer(yp, p_prompt[i], pos_p, None, lp, i)
        ys, (k2, v2, s2, c2) = layer(ys, p_sample[i], pos_s,
                                     (cache_k[i], cache_v[i], state_ret[i], state_conv[i]), lp, i)
        kp.append(k1); ks_.append(k2); vp.append(v1); vs.append(v2)
        rp.append(s1); rs.append(s2); cp.append(c1); cs.append(c2)
    return (yp, ys, jnp.stack(kp), jnp.stack(ks_), jnp.stack(vp), jnp.stack(vs),
            jnp.stack(rp), jnp.stack(rs), jnp.stack(cp), jnp.stack(cs))


_drawn_inputs = setup_inputs


def setup_inputs(seed=0):
    import zlib

    import numpy as np

    out = dict(_drawn_inputs(seed))
    spreads = {}
    factors = {'g_qn': 6.474, 'g_dnorm': 6.877, 'g_ffn': 2.92, 'conv_b': 4.584, 'g_ple': 8.0}
    for name, (base, spread) in spreads.items():
        noise = np.random.default_rng([zlib.crc32(name.encode()), seed]).standard_normal(out[name].shape)
        drawn = base * np.exp(spread * noise) if base else spread * noise
        out[name] = __import__('jax').numpy.asarray(drawn.astype(out[name].dtype))
    for name, factor in factors.items():
        out[name] = (out[name] * factor).astype(out[name].dtype)
    return out
```

```python
import math
from contextlib import ExitStack

import concourse.bass as bass
from concourse import mybir

F32 = mybir.dt.float32
F32R = mybir.dt.float32r
ALU = mybir.AluOpType
ACT = mybir.ActivationFunctionType
AX_X = mybir.AxisListType.X

P = 128
D = 1024
KT = D // P
NP = 1024
NS = 32
NT = NP + NS
PAST = 128
TILES = NP // P + 1
LAST = TILES - 1
THIRD = NT // 3
HEADS = 4
DK, DV = 128, 256
FF = 2816
FT = FF // P
GAP = 2
UW = NT + 2 * GAP
CW = UW - GAP
EPS = 1e-6
LAM_INIT = 0.8 - 0.6 * math.exp(-0.3 * 0)
MASKED = -1e30
SLOTS = 8
RAW = 4
C_RQ, C_RK, C_RV, C_RG, C_DQ, C_DK, C_DV, C_GA = 0, 512, 1024, 2048, 3072, 4096, 5120, 6144
U_GATES = 24
U_RET = U_GATES
U_DIFF = U_RET + 4 * HEADS
U_B = U_DIFF + 6 * HEADS
U_UP = U_B + 24
U_DOWN = U_UP + 2 * FT
U_PLE = U_DOWN + 3 * 24
U_PG = U_PLE + 2
A_B1, A_B2, A_OUT, A_UP = U_GATES, U_GATES + 8, U_GATES + 16, U_GATES + 24
A_PLE = A_UP + 2 * FT
DIFF_STEPS = TILES + 5
L_MIX, L_B1, L_B2, L_OUT, L_FFN, L_DOWN = 0, 8, 16, 24, 32, 40
L_PLE = L_DOWN + 3 * FT
SSQ = (7, 14, 35)
PG_SLOTS = (6, 7, 3)
HC = 2 * P + 4


def rows(i):
    return P if i < LAST else NS


def kernel_program(nc, t):
    with ExitStack() as ctx:
        def sb(name, shape, dt=F32):
            return ctx.enter_context(nc.sbuf_tensor(name, shape, dt))

        def sem(name):
            return ctx.enter_context(nc.semaphore(name))

        def dram(name, shape):
            return nc.dram_tensor(name, shape, F32, kind="Internal").ap()

        w_raw = sb("w_raw", [P, RAW, 8 * P])
        w_hi = sb("w_hi", [P, SLOTS, 8 * P], F32R)
        w_lo = sb("w_lo", [P, SLOTS, 8 * P], F32R)
        a_hi = sb("a_hi", [P, KT * NT], F32R)
        a_lo = sb("a_lo", [P, KT * NT], F32R)
        full = sb("full", [P, KT * NT])
        scr = sb("scr", [P, 6 * UW])
        ident = sb("ident", [P, P])
        ones = sb("ones", [P, P])
        cols = sb("cols", [P, 26])
        convc = sb("convc", [P, 4, 2 * FT])
        convs = sb("convs", [P, 2, 2 * FT])
        u_last = sb("u_last", [P, 2 * FT, 4])
        lamt = sb("lamt", [P, 9])
        eps = sb("eps", [P, 1])
        ps = ctx.enter_context(nc.psum_tensor("ps", [P, 8, 512], F32))

        gates_d = dram("gates_d", [U_GATES, P, NT])
        o_d = dram("o_d", [16, P, NT])
        xt_d = dram("xt_d", [KT, P, NT])
        hid_d = dram("hid_d", [FT, P, NT])

        def ahi(k):
            return a_hi[:, k * NT:(k + 1) * NT]

        def alo(k):
            return a_lo[:, k * NT:(k + 1) * NT]

        def x(k):
            return full[:, k * NT:(k + 1) * NT]

        def row(j, n=NT):
            return scr[:, j * UW:j * UW + n]

        def thirds(v):
            return v.rearrange("p (c n) -> p c n", c=3)

        def acc(n):
            b = 3 * (n % 2)
            return ps[:, b:b + 3, 0:THIRD]

        def wk(w, slot, k):
            return w[:, slot, k * P:(k + 1) * P]

        xin = scr[:, 0:3 * D].rearrange("p (b n) -> p b n", b=3)
        vecs = scr[:, 3 * D:3 * D + 4 * P].rearrange("p (b n) -> p b n", b=4)

        class Carve:
            def __init__(self, tensor, words):
                self.tensor, self.words, self.at = tensor, words, 0

            def take(self, n):
                self.at += n
                assert self.at <= self.words
                return self.tensor[:, self.at - n:self.at]

        f, s = Carve(full, KT * NT), Carve(scr, 6 * UW)
        cos = f.take(8 * 64).rearrange("p (t c) -> p t c", t=8)
        sin = f.take(8 * 64).rearrange("p (t c) -> p t c", t=8)
        gqk = f.take(2 * P).rearrange("p (g c) -> p g c", g=2)
        mask = f.take(2 * P)
        k_t = f.take(2 * (NT + PAST)).rearrange("p (m n) -> p m n", m=2)
        v_tok = f.take((TILES + 1) * DV).rearrange("p (t c) -> p t c", t=TILES + 1)
        nrm = f.take(512)
        a_t = f.take(1024).rearrange("p (b n) -> p b n", b=8)
        kc = f.take(2 * P)
        rope_b = s.take(512)
        qk = s.take(2 * 512).rearrange("p (b n) -> p b n", b=2)
        e0 = s.take(1024)
        e1 = s.take(1024)
        a_w = s.take(1024)
        q_t = s.take(2 * 2 * P).rearrange("p (b m n) -> p b m n", b=2, m=2)
        o_n = s.take(2 * DV).rearrange("p (b n) -> p b n", b=2)
        o_t = s.take(2 * DV).rearrange("p (b m n) -> p b m n", b=2, m=2)
        st = s.take(48)
        hc = full[:, 1536 + 2368 + 2560 + 512:1536 + 2368 + 2560 + 512 + HC]
        kd = k_t[:, 0, 0:3 * P].rearrange("p (b n) -> p b n", b=3)
        s_m = k_t[:, 0, 384:640].rearrange("p (b n) -> p b n", b=2)
        qk_t = k_t[:, 1, 0:512].rearrange("p (b n) -> p b n", b=2)
        q_d = k_t[:, 1, 512:768].rearrange("p (b n) -> p b n", b=2)
        s_p, s_s = e0[:, 0:DV], e0[:, DV:2 * DV]

        names = """const_in vec_in xt_st vec_tr vec_ev lam_m lam_s lam_e lam_d
            x_tr x_ev_a x_ev_d sq_done ssq_done ssq_bc rms_rt rms_inv g_scaled
            w_begun tail_begun pre_done hi_done lo_done w_hi_done w_split acc_done acc_free 
            head_const head_in ret_proj rope_m rope_done kd_done v_done qk_tr qk_ev qd_done
            sc_done sm_done o_done kv_done state_done o_sq o_rt o_inv o_nrm ot_tr ot_ev s_out
            d_in dc_tr dc_ev pa_done pb_done d_sq d_rt d_inv d_nrm d_ropem d_rope d_v d_tr d_ev
            s0_done s1_done m0_done m1_done e0_done e1_done r_inv r_lam t_done a_done
            at0_tr at1_tr at0_ev at1_ev pv_done do_sq do_rt do_inv do_nrm dot_tr dot_ev v_st
            x_add u_pad u_free conv_t silu_done hid_done hid_st u_last_done
            down_done down_free ul_tr ul_ev ul_st ple_in ple_tr ple_hi ple_lo
            sig_done y_mul y_done y_tr y_ev"""
        S = {n: sem(n) for n in names.split()}
        w_landed = [sem(f"w_landed{j}") for j in range(RAW)]
        x_landed = [sem(f"x_landed{j}") for j in range(3)]
        side_in = [sem(f"side_in{j}") for j in range(3)]
        hid_in = [sem(f"hid_in{j}") for j in range(4)]
        gate_st = [sem(f"gate_st{j}") for j in range(2)]
        ot_st = [sem(f"ot_st{j}") for j in range(2)]
        dot_st = [sem(f"dot_st{j}") for j in range(2)]
        k_st = [sem(f"k_st{j}") for j in range(2)]
        y_st = [sem(f"y_st{j}") for j in range(2)]

        w_in = t["w_in"][0].rearrange("(k p) n -> p k n", p=P)
        w_of = {n: t[n][0].rearrange("(k p) n -> p k n", p=P)
                for n in ("w_ret_br", "w_da_br", "w_out", "w_up", "w_down", "w_ple_gate", "w_ple")}
        lam = lamt[:, 8:9]

        def bcast(v, n):
            return v.unsqueeze(1).broadcast_to([v.shape[0], n, v.shape[1]])

        def side(q):
            return row(3 + q % 3)

        def hid_piece(k):
            at = (2 + (k // 3) % 4) * UW + (k % 3) * THIRD
            return scr[:, at:at + THIRD]

        ple_in = scr[:, 2 * UW:2 * UW + TILES * 2 * P].rearrange("p (i c) -> p i c", i=TILES)
        ple_hi = w_hi[:, 0:3, :].rearrange("p s c -> p (s c)")[:, 0:2 * NT]
        ple_lo = w_lo[:, 0:3, :].rearrange("p s c -> p (s c)")[:, 0:2 * NT]
        y_tok = scr[:, 2 * UW:2 * UW + 2 * TILES * P].rearrange("p (b i c) -> p b i c", b=2, i=TILES)
        s_bank = ps[:, 5:7, :].rearrange("p b n -> p (b n)")

        def ple_part(v, b):
            n = 2 * P if b < 4 else NS
            return v.rearrange("p (k n) -> p k n", k=2)[:, :, 2 * b * P:2 * b * P + n]

        def ple_block(b):
            n = 2 * P if b < 4 else NS
            return ps[:, 6 + b % 2, :].rearrange("p (k n) -> p k n", k=2)[:, :, 0:n]

        u_g, u_v = scr[:, 3 * UW:4 * UW], scr[:, 4 * UW:5 * UW]

        block = ctx.enter_context(nc.Block())

        @block.sync
        def _(sp):
            for at, n, name in ((0, 8, "g_mix"), (8, 8, "g_ffn"), (16, 8, "g_ple"), (24, 2, "g_dnorm")):
                sp.dma_start(vecs[at:at + n, 0, :], t[name][0].rearrange("(r c) -> r c", c=P)).then_inc(S["vec_in"], 16)
            taps = t["conv_w"][0].rearrange("w (j c) -> w j c", c=P)
            for w in range(3):
                sp.dma_start(vecs[44 * (w % 2):44 * (w % 2) + 44, 1 + w // 2, :], taps[w]).then_inc(S["vec_in"], 16)
            sp.dma_start(vecs[44:88, 2, :], t["conv_b"][0].rearrange("(j c) -> j c", c=P)).then_inc(S["vec_in"], 16)
            past = t["state_conv"][0, 0].rearrange("w (j c) -> w j c", c=P)
            for w in range(2):
                sp.dma_start(vecs[44 * w:44 * w + 44, 3, :], past[w]).then_inc(S["vec_in"], 16)
            for n, name in enumerate(("lam_q1", "lam_q2", "lam_k1", "lam_k2")):
                sp.dma_start(lamt[:, n:n + 1], t[name][0].rearrange("(c a) -> c a", a=1)).then_inc(S["vec_in"], 16)
            sp.dma_start(ident[:, :], t["c_ident"]).then_inc(S["const_in"], 16)

            def load_x(i):
                if i >= 3:
                    sp.wait_ge(S["x_tr"], i - 2)
                src = t["x_prompt"][0, i * P:(i + 1) * P, :] if i < LAST else t["x_sample"][0]
                sp.dma_start(xin[0:rows(i), i % 3, :], src).then_inc(x_landed[i % 3], 16)

            def weights(before, j, src, wait=True):
                if wait:
                    sp.wait_ge(S["w_split"], before + (j - 3))
                dst = w_raw[:, j % RAW, 0:src.shape[1] * src.shape[2]]
                sp.dma_start(dst.rearrange("p (k c) -> p k c", k=src.shape[1]), src).then_inc(w_landed[j % RAW], 16)

            for i in range(3):
                load_x(i)
            for j in range(RAW):
                weights(0, j, w_in[:, :, C_RG + j * P:C_RG + (j + 1) * P], wait=False)
            for i in range(3, TILES):
                load_x(i)
            for j in range(RAW, 8):
                weights(0, j, w_in[:, :, C_RG + j * P:C_RG + (j + 1) * P])
            with sp.Fori(0, 4) as g:
                for j in range(4):
                    weights(g * 4 + 8, j, w_in[:, :, bass.ds(g * (4 * P) + (C_GA + j * P), P)])
            with sp.Fori(0, HEADS) as h:
                for j, (c, step) in enumerate(((C_RQ, DK), (C_RK, DK), (C_RV, DV), (C_RV + P, DV))):
                    weights(h * 4 + U_RET, j, w_in[:, :, bass.ds(h * step + c, P)])
            with sp.Fori(0, HEADS // 2) as g:
                for h in range(2):
                    for j, c in enumerate((C_DQ, C_DQ + P, C_DK, C_DK + P, C_DV, C_DV + P)):
                        weights(g * 12 + U_DIFF, 6 * h + j, w_in[:, :, bass.ds(g * (4 * P) + (c + h * 2 * P), P)])
            for b, name in enumerate(("w_ret_br", "w_da_br", "w_out")):
                with sp.Fori(0, 2) as g:
                    for j in range(4):
                        weights(g * 4 + (U_B + 8 * b), j, w_of[name][:, :, bass.ds(g * (4 * P) + j * P, P)])
            with sp.Fori(0, FT // 2) as g:
                for j in range(4):
                    c = (j % 2) * FF + (j // 2) * P
                    weights(g * 4 + U_UP, j, w_of["w_up"][:, :, bass.ds(g * (2 * P) + c, P)])
            with sp.Fori(0, 3) as third:
                with sp.Fori(0, 2) as g:
                    for j in range(12):
                        k = 8 * (j % 3)
                        weights(third * 24 + g * 12 + U_DOWN, j,
                                w_of["w_down"][:, k:min(k + 8, FT), bass.ds(g * (4 * P) + (j // 3) * P, P)])
            for j in range(2):
                weights(U_PLE, j, w_of["w_ple"][:, :, j * 512:(j + 1) * 512])
            for j in range(8):
                weights(U_PG - 2, j + 2, w_of["w_ple_gate"][:, :, j * P:(j + 1) * P])

        @block.gpsimd
        def _(pool):
            def split(before, j, slot, words=8 * P):
                landed = (before + (j - j % RAW)) * 4 + 16
                pool.wait_ge(w_landed[j % RAW], landed)
                pool.sem_inc(S["w_begun"], 1)
                raw, hi, lo = w_raw[:, j % RAW, 0:words], w_hi[:, slot, 0:words], w_lo[:, slot, 0:words]
                pool.tensor_scalar(hi, raw, 1.0, 0.0, ALU.mult, ALU.add).then_inc(S["w_hi_done"], 1)
                pool.wait_ge(S["w_hi_done"], before + (j + 1))
                pool.tensor_tensor(lo, raw, hi.bitcast(F32), ALU.subtract).then_inc(S["w_split"], 1)

            for j in range(8):
                split(0, j, j)
            with pool.Fori(1, 3) as g:
                for j in range(8):
                    pool.wait_ge(S["acc_done"], g * 8 + (j - 7))
                    split(g * 8, j, j)
            pool.wait_ge(S["acc_done"], U_GATES)
            for j in range(4):
                split(U_RET, j, j)
            with pool.Fori(1, HEADS) as h:
                pool.wait_ge(S["ret_proj"], h * TILES)
                for j in range(4):
                    split(h * 4 + U_RET, j, j)
            pool.wait_ge(S["ret_proj"], HEADS * TILES)
            for j in range(6):
                split(U_DIFF, j, j)
            for h in range(1, HEADS):
                pool.wait_ge(S["pb_done"], h * TILES)
                for j in range(6):
                    split(U_DIFF, 6 * h + j, j)
            pool.wait_ge(S["pb_done"], HEADS * TILES)
            for j in range(8):
                split(U_B, j, j)
            with pool.Fori(1, (U_DOWN - U_B) // 8) as g:
                for j in range(8):
                    pool.wait_ge(S["acc_done"], g * 8 + (A_B1 + j - 7))
                    split(g * 8 + U_B, j, j)
            for j in range(U_DOWN - 4, U_DOWN):
                pool.wait_ge(S["acc_done"], j - U_B + A_B1 - 7)
                split(0, j, j % SLOTS)
            def down_units(before, tiles, first):
                for j in range(24):
                    if first and j < 8:
                        pool.wait_ge(S["acc_done"], A_PLE - 7 + j)
                    else:
                        pool.wait_ge(S["down_done"], tiles + ((j - 8) // 3 + 1))
                    split(before, j, (U_DOWN + j) % SLOTS, words=8 * P if j % 3 < 2 else (FT - 16) * P)
            down_units(U_DOWN, 0, True)
            with pool.Fori(1, 3) as third:
                down_units(third * 24 + U_DOWN, third * 8, False)
            for j in range(2):
                pool.wait_ge(S["down_done"], 24)
                split(U_PLE, j, 4 + j)
            for m in range(8):
                if m >= 3:
                    pool.wait_ge(S["acc_done"], A_PLE + 2 * (m - 3) + 2)
                split(U_PLE, 2 + m, PG_SLOTS[m % 3])

        @block.tensor
        def _(pe):
            def three(out, lhs, rhs, start, stop):
                pe.matmul(out, lhs[0], rhs[0], start=start, stop=False)
                pe.matmul(out, lhs[0], rhs[1], start=False, stop=False)
                return pe.matmul(out, lhs[1], rhs[0], start=False, stop=stop)

            def feature_tile(n, slot, ready=None):
                for k in range(KT):
                    if ready is not None:
                        pe.wait_ge(S["lo_done"], ready + k + 1)
                    for c in range(3):
                        cut = slice(k * NT + c * THIRD, k * NT + (c + 1) * THIRD)
                        last = three(acc(n)[:, c, :], (wk(w_hi, slot, k), wk(w_lo, slot, k)),
                                     (a_hi[:, cut], a_lo[:, cut]), k == 0, k == KT - 1)
                return last

            pe.wait_ge(S["const_in"], 16)
            pe.wait_ge(S["vec_in"], 16 * 14)
            for b, r in enumerate((26, 88, 88, 88)):
                last = pe.transpose(ps[:, 7, b * P:b * P + r], vecs[0:r, b, :], ident[0:r, 0:r])
            last.then_inc(S["vec_tr"], 1)
            pe.wait_ge(S["lam_m"], 2)
            pe.matmul(ps[:, 6, 0:2], ones[:, :], lamt[:, 4:6], start=True, stop=True).then_inc(S["lam_s"], 1)
            for i in range(TILES):
                r = rows(i)
                pe.wait_ge(x_landed[i % 3], 16 * (i // 3 + 1))
                if i >= 2:
                    pe.wait_ge(S["x_ev_a"], i - 1)
                    pe.wait_ge(S["x_ev_d"], i - 1)
                for k in range(KT):
                    last = pe.transpose(ps[:, 2 * (i % 2) + k // 4, (k % 4) * P:(k % 4) * P + r],
                                        xin[0:r, i % 3, k * P:(k + 1) * P], ident[0:r, 0:r])
                last.then_inc(S["x_tr"], 1)

            def sum_over_features(n):
                pe.wait_ge(S["ssq_done"], n)
                for c in range(3):
                    last = pe.matmul(acc(0)[:, c, :], ones[:, :], row(0)[:, c * THIRD:(c + 1) * THIRD],
                                     start=True, stop=True)
                last.then_inc(S["ssq_bc"], 1)

            pe.wait_ge(S["x_ev_a"], TILES)
            pe.wait_ge(S["x_ev_d"], TILES)
            sum_over_features(SSQ[0])

            for j in range(8):
                pe.wait_ge(S["w_split"], j + 1)
                if j >= 2:
                    pe.wait_ge(S["acc_free"], j - 1)
                feature_tile(j, j, ready=L_MIX if j == 0 else None).then_inc(S["acc_done"], 1)
            with pe.Fori(1, 3) as g:
                for j in range(8):
                    pe.wait_ge(S["w_split"], g * 8 + (j + 1))
                    pe.wait_ge(S["acc_free"], g * 8 + (j - 1))
                    feature_tile(j, j).then_inc(S["acc_done"], 1)
            pe.wait_ge(S["acc_free"], U_GATES)

            def project(bank, i, s0, s1):
                r, n = rows(i), (s1 - s0) * P
                out = ps[0:r, bank, 0:n].rearrange("p (s c) -> p s c", c=P)
                for k in range(KT):
                    cut = slice(k * NT + i * P, k * NT + i * P + r)
                    last = three(out, (a_hi[:, cut], a_lo[:, cut]),
                                 (w_hi[:, s0:s1, k * P:(k + 1) * P], w_lo[:, s0:s1, k * P:(k + 1) * P]),
                                 k == 0, k == KT - 1)
                return last

            def begun(i):
                if i == LAST:
                    pe.sem_inc(S["tail_begun"], 1)

            with pe.Fori(0, HEADS) as h:
                c9 = h * TILES
                for step in range(TILES + 4):
                    i = step
                    if i < TILES:
                        if i == 0:
                            pe.wait_ge(S["w_split"], h * 4 + (U_RET + 4))
                        if i >= 3:
                            pe.wait_ge(S["rope_done"], h * (2 * TILES) + 2 * (i - 2))
                        project(i % 3, i, 0, 4).then_inc(S["ret_proj"], 1)
                    i = step - 1
                    if 0 <= i < TILES:
                        r = rows(i)
                        pe.wait_ge(S["rope_done"], h * (2 * TILES) + 2 * (i + 1))
                        if i >= 1:
                            pe.wait_ge(S["qk_ev"], c9 + i)
                        begun(i)
                        for m in range(2):
                            last = pe.transpose(ps[:, 4, m * P:m * P + r], qk[0:r, i % 2, m * P:(m + 1) * P],
                                                ident[0:r, 0:r])
                        last.then_inc(S["qk_tr"], 1)
                    i = step - 2
                    if 0 <= i < TILES:
                        r = rows(i)
                        pe.wait_ge(S["qk_ev"], c9 + (i + 1))
                        if i >= 1:
                            pe.wait_ge(S["sm_done"], c9 + i)
                        begun(i)
                        pe.matmul(ps[0:r, 5, 0:r], qk_t[:, i % 2, P:P + r], qk_t[:, i % 2, 0:r],
                                  start=True, stop=True).then_inc(S["sc_done"], 1)
                    i = step - 3
                    if 0 <= i < TILES:
                        r = rows(i)
                        pe.wait_ge(S["sm_done"], c9 + (i + 1))
                        pe.wait_ge(S["v_done"], c9 + (i + 1))
                        pe.wait_ge(S["kd_done"], c9 + (i + 1))
                        pe.wait_ge(S["qd_done"], c9 + (i + 1))
                        if i >= 1:
                            pe.wait_ge(S["o_nrm"], c9 + i)
                            pe.wait_ge(S["state_done"], c9 + i)
                        else:
                            pe.wait_ge(S["head_in"], h * 32 + 32)
                        begun(i)
                        out = ps[0:r, 6, 0:DV]
                        last = pe.matmul(out, s_m[0:r, i % 2, 0:r], v_tok[0:r, i, :], start=True, stop=i == 0)
                        if i:
                            last = pe.matmul(out, q_d[:, i % 2, 0:r], s_p if i < LAST else s_s, start=False, stop=True)
                        last.then_inc(S["o_done"], 1)
                        pe.matmul(ps[:, 7, 0:DV], kd[0:r, i % 3, :], v_tok[0:r, i, :],
                                  start=True, stop=True).then_inc(S["kv_done"], 1)
                    i = step - 4
                    if 0 <= i < TILES:
                        r = rows(i)
                        pe.wait_ge(S["o_nrm"], c9 + (i + 1))
                        if i >= 1:
                            pe.wait_ge(S["ot_ev"], c9 + i)
                        begun(i)
                        for m in range(2):
                            last = pe.transpose(ps[:, 3, m * P:m * P + r],
                                                o_n[0:r, i % 2, m * P:(m + 1) * P], ident[0:r, 0:r])
                        last.then_inc(S["ot_tr"], 1)
                pe.wait_ge(S["ot_ev"], c9 + TILES)
                pe.wait_ge(S["state_done"], c9 + TILES)

            with pe.Fori(0, HEADS) as h:
                c9 = h * TILES
                pe.wait_ge(S["d_in"], h * 32 + 32)
                for m in range(2):
                    last = pe.transpose(ps[:, 4, m * P:(m + 1) * P], kc[:, m * P:(m + 1) * P], ident[:, :])
                last.then_inc(S["dc_tr"], 1)
                for step in range(DIFF_STEPS):
                    def scores(m, i):
                        keys, first = (P * (i + 1), 0) if i < LAST else (NS + PAST, NP)
                        r = rows(i)
                        for b in range(0, keys, 512):
                            n = min(512, keys - b)
                            diag = i < LAST and b + n == keys
                            last = pe.matmul(ps[0:r, 5 + b // 512, 0:n], q_t[:, i % 2, m, 0:r],
                                             k_t[:, m, first + b:first + b + n], start=True, stop=not diag)
                            if diag:
                                last = pe.matmul(ps[0:r, 5 + b // 512, n - P:n], mask[0:1, 0:P], mask[0:1, P:2 * P],
                                                 start=False, stop=True)
                        return last

                    def blocks(i):
                        if i < LAST:
                            return [(P, b * P, b) for b in range(i + 1)]
                        return [(NS, 0, LAST), (P, NS, TILES)]

                    def transpose_a(i, b0, b1):
                        r = rows(i)
                        for b in range(b0, b1):
                            n, c, _ = blocks(i)[b]
                            last = pe.transpose(ps[0:n, 4, (b % 4) * P:(b % 4) * P + r], a_w[0:r, c:c + n],
                                                ident[0:r, 0:r])
                        return last

                    def weigh_v(i, b0, b1):
                        r, every = rows(i), len(blocks(i))
                        for b in range(b0, b1):
                            n, _, vt = blocks(i)[b]
                            last = pe.matmul(ps[0:r, 7, 0:DV], a_t[0:n, b, 0:r], v_tok[0:n, vt, :],
                                             start=b == 0, stop=b == every - 1)
                        return last

                    i = step - 2
                    if 0 <= i < TILES:
                        pe.wait_ge(S["d_ev"], h * (2 * TILES) + 2 * (i + 1))
                        if i == LAST:
                            pe.wait_ge(S["dc_ev"], h + 1)
                        if i >= 1:
                            pe.wait_ge(S["e1_done"], c9 + i)
                        begun(i)
                        scores(0, i).then_inc(S["s0_done"], 1)
                    i = step - 3
                    if 0 <= i < TILES:
                        every = len(blocks(i))
                        pe.wait_ge(S["a_done"], c9 + (i + 1))
                        if i + 1 < TILES:
                            pe.wait_ge(S["d_ev"], h * (2 * TILES) + 2 * (i + 2))
                        begun(i)
                        transpose_a(i, 0, min(4, every)).then_inc(S["at0_tr"], 1)
                    i = step
                    if i < TILES:
                        if i == 0:
                            pe.wait_ge(S["w_split"], h * 6 + (U_DIFF + 3))
                        if i >= 2:
                            pe.wait_ge(S["d_nrm"], h * (4 * TILES) + 4 * (i - 1))
                            pe.wait_ge(S["d_v"], c9 + (i - 1))
                        project(2 * (i % 2), i, 0, 3).then_inc(S["pa_done"], 1)
                    i = step - 2
                    if 0 <= i < TILES:
                        pe.wait_ge(S["e0_done"], c9 + (i + 1))
                        begun(i)
                        scores(1, i).then_inc(S["s1_done"], 1)
                    i = step - 3
                    if 0 <= i < TILES:
                        pe.wait_ge(S["at0_ev"], c9 + (i + 1))
                        if i >= 1:
                            pe.wait_ge(S["do_nrm"], c9 + i)
                        if i >= 2:
                            pe.wait_ge(S["dot_ev"], h * (2 * TILES) + 2 * (i - 1))
                        begun(i)
                        last = weigh_v(i, 0, min(4, every))
                        if every <= 4:
                            last.then_inc(S["pv_done"], 1)
                        else:
                            transpose_a(i, 4, every).then_inc(S["at1_tr"], 1)
                    i = step
                    if i < TILES:
                        if i == 0:
                            pe.wait_ge(S["w_split"], h * 6 + (U_DIFF + 6))
                        project(2 * (i % 2) + 1, i, 3, 6).then_inc(S["pb_done"], 1)
                    i = step - 1
                    if 0 <= i < TILES:
                        r = rows(i)
                        pe.wait_ge(S["d_rope"], h * (2 * TILES) + 2 * (i + 1))
                        if i == 0:
                            pe.wait_ge(S["dc_ev"], h + 1)
                        if 4 <= step - 3 < LAST:
                            pe.wait_ge(S["at1_ev"], h * 4 + (step - 3 - 3))
                        begun(i)
                        for m in range(4):
                            last = pe.transpose(ps[:, 4, m * P:m * P + r], qk[0:r, i % 2, m * P:(m + 1) * P],
                                                ident[0:r, 0:r])
                        last.then_inc(S["d_tr"], 1)
                    i = step - 3
                    if 0 <= i < TILES and every > 4:
                        pe.wait_ge(S["at1_ev"], h * 4 + (i - 3))
                        weigh_v(i, 4, every).then_inc(S["pv_done"], 1)
                    i = step - 4
                    if 0 <= i < TILES:
                        r = rows(i)
                        pe.wait_ge(S["do_nrm"], c9 + (i + 1))
                        if i >= 1:
                            pe.wait_ge(S["dot_ev"], h * (2 * TILES) + 2 * i)
                        begun(i)
                        for m in range(2):
                            last = pe.transpose(ps[:, 7, (2 + m) * P:(2 + m) * P + r],
                                                o_n[0:r, i % 2, m * P:(m + 1) * P], ident[0:r, 0:r])
                        last.then_inc(S["dot_tr"], 1)
                pe.wait_ge(S["dot_ev"], h * (2 * TILES) + 2 * TILES)

            for b in range(3):
                for j in range(8):
                    n = A_B1 + 8 * b + j
                    pe.wait_ge(S["w_split"], U_B + 8 * b + j + 1)
                    pe.wait_ge(S["acc_free"], n - 1)
                    feature_tile(n, j, ready=L_B1 + 8 * b if j == 0 else None).then_inc(S["acc_done"], 1)
            pe.wait_ge(S["acc_free"], A_UP)
            sum_over_features(SSQ[1])
            pe.wait_ge(S["lo_done"], L_FFN + KT)
            with pe.Fori(0, 2 * FT // 8) as g:
                for j in range(8):
                    pe.wait_ge(S["w_split"], g * 8 + (U_UP + j + 1))
                    pe.wait_ge(S["acc_free"], g * 8 + (A_UP + j - 1))
                    feature_tile(j, j).then_inc(S["acc_done"], 1)
            for j in range(2 * FT - 4, 2 * FT):
                pe.wait_ge(S["w_split"], U_UP + j + 1)
                pe.wait_ge(S["acc_free"], A_UP + j - 1)
                feature_tile(j, j % SLOTS).then_inc(S["acc_done"], 1)
            pe.wait_ge(S["u_last_done"], 2 * FT)
            pe.wait_ge(S["acc_free"], A_PLE)
            for b in range(2):
                flat = u_last[:, b * FT:(b + 1) * FT, :].rearrange("p j w -> p (j w)")
                last = pe.transpose(ps[0:4 * FT, 7, b * P:(b + 1) * P], flat, ident[:, :])
            last.then_inc(S["ul_tr"], 1)
            pe.wait_ge(S["ul_ev"], 1)
            with pe.Fori(0, 3) as third:
                for m in range(8):
                    pe.wait_ge(S["down_free"], third * 8 + (m + 1))
                    for k in range(FT):
                        if k % 8 == 0:
                            pe.wait_ge(S["w_split"], third * 24 + (U_DOWN + 3 * m + k // 8 + 1))
                        if m == 0:
                            pe.wait_ge(S["lo_done"], third * FT + (L_DOWN + k + 1))
                        slot = (U_DOWN + 3 * m + k // 8) % SLOTS
                        cut = slice(k * THIRD, (k + 1) * THIRD)
                        last = three(ps[:, m, 0:THIRD], (wk(w_hi, slot, k % 8), wk(w_lo, slot, k % 8)),
                                     (a_hi[:, cut], a_lo[:, cut]), k == 0, k == FT - 1)
                    last.then_inc(S["down_done"], 1)
            sum_over_features(SSQ[2])

            def out_rows(m):
                pe.wait_ge(S["y_done"], m + 1)
                for part, (i0, i1) in enumerate(((0, 4), (4, 8), (8, 9))):
                    need = 3 * m + (0, 0, 1)[part]
                    if need:
                        pe.wait_ge(S["y_ev"], need)
                    for i in range(i0, i1):
                        r = rows(i)
                        last = pe.transpose(ps[0:r, 6 + part % 2, (i % 4) * P:(i % 4 + 1) * P],
                                            x(m)[:, i * P:i * P + r], ident[:, :])
                    last.then_inc(S["y_tr"], 1)

            pe.wait_ge(S["ple_in"], 32)
            for b in range(5):
                if b >= 2:
                    pe.wait_ge(S["ple_lo"], b - 1)
                for i in range(2 * b, min(2 * b + 2, TILES)):
                    r = rows(i)
                    for k in range(2):
                        at = (2 * k + i % 2) * P
                        last = pe.transpose(ps[:, 6 + b % 2, at:at + r], ple_in[0:r, i, k * P:(k + 1) * P],
                                            ident[0:r, 0:r])
                last.then_inc(S["ple_tr"], 1)
            pe.wait_ge(S["ple_lo"], 5)
            for m in range(8):
                n = A_PLE + 2 * m
                if m == 0:
                    pe.wait_ge(S["w_split"], U_PLE + 2)
                    pe.wait_ge(S["rms_rt"], 3)
                else:
                    pe.wait_ge(S["y_mul"], m)
                for k in range(2):
                    at = k * 512 + (m % 4) * P
                    for c in range(3):
                        cut = slice(k * NT + c * THIRD, k * NT + (c + 1) * THIRD)
                        last = three(acc(0)[:, c, :],
                                     (w_hi[:, 4 + m // 4, at:at + P], w_lo[:, 4 + m // 4, at:at + P]),
                                     (ple_hi[:, cut], ple_lo[:, cut]), k == 0, k == 1)
                last.then_inc(S["acc_done"], 1)
                pe.wait_ge(S["w_split"], U_PG + m + 1)
                if m:
                    pe.wait_ge(S["sig_done"], m)
                feature_tile(1, PG_SLOTS[m % 3], ready=L_PLE if m == 0 else None).then_inc(S["acc_done"], 1)
                if m:
                    out_rows(m - 1)
            out_rows(7)

        @block.scalar
        def _(act):
            act.wait_ge(S["lam_s"], 1)
            act.activation(lamt[:, 6:8], ps[:, 6, 0:2], ACT.Exp).then_inc(S["lam_e"], 1)
            full_k = full[:, :].rearrange("p (k n) -> p k n", k=KT)
            for i in range(TILES):
                r = rows(i)
                act.wait_ge(S["x_tr"], i + 1)
                act.copy(full_k[:, 0:4, i * P:i * P + r],
                         ps[:, 2 * (i % 2), :].rearrange("p (k c) -> p k c", k=4)[:, :, 0:r]).then_inc(S["x_ev_a"], 1)
            act.wait_ge(S["x_ev_a"], TILES)
            act.wait_ge(S["x_ev_d"], TILES)
            act.dma_start(xt_d.rearrange("k p n -> p k n"), full_k).then_inc(S["xt_st"], 16)

            def square(k, before, adds):
                if k >= 2:
                    act.wait_ge(S["ssq_done"], adds + k - 1)
                act.activation(row(1) if k else row(0), x(k), ACT.Square).then_inc(S["sq_done"], 1)

            for k in range(KT):
                square(k, 0, 0)

            def root_of_mean():
                act.activation(thirds(row(0)), acc(0), ACT.Sqrt, bias=eps[:, 0:1], scale=1.0 / D).then_inc(S["rms_rt"], 1)

            def hi_of_scaled(split0, pre0):
                for k in range(KT):
                    act.wait_ge(S["pre_done"], pre0 + k + 1)
                    act.activation(ahi(k), row(1 + k % 2), ACT.Copy).then_inc(S["hi_done"], 1)

            act.wait_ge(S["ssq_bc"], 1)
            root_of_mean()
            hi_of_scaled(L_MIX, 0)

            def gate(before, j, func, ring=True):
                act.wait_ge(S["acc_done"], before + (j + 1))
                if ring:
                    act.wait_ge(gate_st[j], before * 8)
                act.activation(thirds(row(3 + j)), acc(j), func).then_inc(S["acc_free"], 1)
                act.wait_ge(S["acc_free"], before + (j + 1))
                act.dma_start(gates_d[bass.ds(before + j, 1)].rearrange("k p n -> p (k n)"), row(3 + j)).then_inc(gate_st[j], 16)

            for j in range(2):
                gate(0, j, ACT.Silu, ring=False)
            with act.Fori(1, 4) as g:
                for j in range(2):
                    gate(g * 2, j, ACT.Silu)
            with act.Fori(4, 12) as g:
                for j in range(2):
                    gate(g * 2, j, ACT.Sigmoid)
            act.wait_ge(gate_st[0], 12 * 16)
            act.wait_ge(gate_st[1], 12 * 16)

            act.wait_ge(S["xt_st"], 16)
            act.wait_ge(S["lo_done"], KT)
            act.dma_start(cos, t["c_cos"]).then_inc(S["head_const"], 16)
            act.dma_start(sin, t["c_sin"]).then_inc(S["head_const"], 16)
            act.dma_start(gqk[:, 0, :], t["g_qn"][0].partition_broadcast(P)).then_inc(S["head_const"], 16)
            act.dma_start(gqk[:, 1, :], t["g_kn"][0].partition_broadcast(P)).then_inc(S["head_const"], 16)
            act.dma_start(mask[0:1, :], t["c_mask"]).then_inc(S["head_const"], 16)

            def root(i, sq, rt, dim, n, before, done):
                r = rows(i)
                act.wait_ge(sq, before)
                act.activation(st[0:r, rt:rt + n], st[0:r, dim[0]:dim[0] + n], ACT.Sqrt, bias=eps[0:r, 0:1],
                               scale=1.0 / dim[1]).then_inc(done, 1)

            with act.Fori(0, HEADS) as h:
                c9 = h * TILES
                act.dma_start(hc, t["c_ret"][bass.ds(h, 1)].rearrange("h p c -> p (h c)")).then_inc(S["head_in"], 16)
                act.dma_start(s_s, t["state_ret"][0, 0][bass.ds(h, 1)].rearrange("h p c -> p (h c)")).then_inc(S["head_in"], 16)
                for step in range(TILES + 4):
                    i = step
                    if i < TILES:
                        r = rows(i)
                        act.wait_ge(S["ret_proj"], c9 + (i + 1))
                        act.copy(v_tok[0:r, i, :], ps[0:r, i % 3, 2 * P:4 * P]).then_inc(S["v_done"], 1)
                    i = step - 1
                    if 0 <= i < TILES:
                        r = rows(i)
                        act.wait_ge(S["qk_tr"], c9 + (i + 1))
                        if i >= 2:
                            act.wait_ge(S["sc_done"], c9 + (i - 1))
                            act.wait_ge(S["qd_done"], c9 + (i - 1))
                        act.copy(qk_t[:, i % 2, :].rearrange("p (m n) -> p m n", m=2)[:, :, 0:r],
                                 ps[:, 4, 0:2 * P].rearrange("p (m n) -> p m n", m=2)[:, :, 0:r]).then_inc(S["qk_ev"], 1)
                    i = step - 3
                    if 0 <= i < TILES:
                        r, b = rows(i), i % 2
                        act.wait_ge(S["o_done"], c9 + (i + 1))
                        if i >= 2:
                            act.wait_ge(S["ot_tr"], c9 + (i - 1))
                        act.activation(o_n[0:r, b, :], ps[0:r, 6, 0:DV], ACT.Square,
                                       accum_out=st[0:r, b:b + 1]).then_inc(S["o_sq"], 1)
                        act.wait_ge(S["o_sq"], c9 + (i + 1))
                        act.activation(st[0:r, 2 + b:3 + b], st[0:r, b:b + 1], ACT.Sqrt, bias=eps[0:r, 0:1],
                                       scale=1.0 / DV).then_inc(S["o_rt"], 1)
                        act.wait_ge(S["o_inv"], c9 + (i + 1))
                        act.activation(o_n[0:r, b, :], ps[0:r, 6, 0:DV], ACT.Copy,
                                       scale=st[0:r, 4 + b:5 + b]).then_inc(S["o_nrm"], 1)
                    i = step - 4
                    if 0 <= i < TILES:
                        r, b = rows(i), i % 2
                        act.wait_ge(S["ot_tr"], c9 + (i + 1))
                        if i >= 2:
                            act.wait_ge(ot_st[b], h * (16 * (5 - b)) + 16 * (i // 2))
                        act.copy(o_t[:, b, :, 0:r],
                                 ps[:, 3, 0:2 * P].rearrange("p (m n) -> p m n", m=2)[:, :, 0:r]).then_inc(S["ot_ev"], 1)
                        act.wait_ge(S["ot_ev"], c9 + (i + 1))
                        act.dma_start(o_d[bass.ds(h * 2, 2), :, i * P:i * P + r].rearrange("m p n -> p m n"),
                                      o_t[:, b, :, 0:r]).then_inc(ot_st[b], 16)
                for i, s_x, name in ((LAST - 1, s_p, "ret_prompt"), (LAST, s_s, "ret_sample")):
                    act.wait_ge(S["state_done"], c9 + (i + 1))
                    act.dma_start(t[name][0, 0][bass.ds(h, 1)].rearrange("h p c -> p (h c)"), s_x).then_inc(S["s_out"], 16)
                act.wait_ge(S["s_out"], h * 32 + 32)
                act.wait_ge(ot_st[0], h * (16 * 5) + 16 * 5)
                act.wait_ge(ot_st[1], h * (16 * 4) + 16 * 4)

            with act.Fori(0, HEADS) as h:
                c9 = h * TILES
                act.dma_start(kc, t["cache_k"][0, 0][:, bass.ds(h, 1)].rearrange("t h m d -> t (h m d)")).then_inc(S["d_in"], 16)
                act.dma_start(v_tok[:, TILES, :], t["cache_v"][0, 0][:, bass.ds(h, 1)].rearrange("t h d -> t (h d)")).then_inc(S["d_in"], 16)
                for step in range(DIFF_STEPS):
                    i = step - 4
                    if 0 <= i < TILES:
                        r, b = rows(i), i % 2
                        act.wait_ge(S["pv_done"], c9 + (i + 1))
                        if i >= 1:
                            act.wait_ge(S["dot_tr"], c9 + i)
                        act.activation(o_n[0:r, b, :], ps[0:r, 7, 0:DV], ACT.Square,
                                       accum_out=st[0:r, b:b + 1]).then_inc(S["do_sq"], 1)
                    i = step - 1
                    if 0 <= i < TILES:
                        r, b = rows(i), i % 2
                        act.wait_ge(S["pa_done"], c9 + (i + 1))
                        if i >= 1:
                            act.wait_ge(S["d_rope"], h * (2 * TILES) + 2 * i)
                        for m in range(4):
                            if m == 3:
                                act.wait_ge(S["pb_done"], c9 + (i + 1))
                            bank, at = (2 * b, m * P) if m < 3 else (2 * b + 1, 0)
                            act.activation(nrm[0:r, m * P:(m + 1) * P], ps[0:r, bank, at:at + P], ACT.Square,
                                           accum_out=st[0:r, 8 + 4 * b + m:9 + 4 * b + m]).then_inc(S["d_sq"], 1)
                    i = step - 4
                    if 0 <= i < TILES:
                        r, b = rows(i), i % 2
                        act.wait_ge(S["do_sq"], c9 + (i + 1))
                        act.activation(st[0:r, 2 + b:3 + b], st[0:r, b:b + 1], ACT.Sqrt, bias=eps[0:r, 0:1],
                                       scale=1.0 / DV).then_inc(S["do_rt"], 1)
                    i = step - 1
                    if 0 <= i < TILES:
                        r, b = rows(i), i % 2
                        act.wait_ge(S["d_sq"], h * (4 * TILES) + 4 * (i + 1))
                        act.activation(st[0:r, 16 + 4 * b:20 + 4 * b], st[0:r, 8 + 4 * b:12 + 4 * b], ACT.Sqrt,
                                       bias=eps[0:r, 0:1], scale=1.0 / DK).then_inc(S["d_rt"], 1)
                        act.copy(v_tok[0:r, i, :], ps[0:r, 2 * b + 1, P:3 * P]).then_inc(S["d_v"], 1)
                        act.wait_ge(S["d_v"], c9 + (i + 1))
                        out = t["new_v_prompt"][0, 0, i * P:(i + 1) * P] if i < LAST else t["new_v_sample"][0, 0]
                        act.dma_start(out[:, bass.ds(h, 1)].rearrange("t h d -> t (h d)"), v_tok[0:r, i, :]).then_inc(S["v_st"], 16)
                    i = step - 4
                    if 0 <= i < TILES:
                        r, b = rows(i), i % 2
                        act.wait_ge(S["do_inv"], c9 + (i + 1))
                        act.activation(o_n[0:r, b, :], ps[0:r, 7, 0:DV], ACT.Copy,
                                       scale=st[0:r, 4 + b:5 + b]).then_inc(S["do_nrm"], 1)
                    i = step - 5
                    if 0 <= i < TILES:
                        r, b = rows(i), i % 2
                        act.wait_ge(S["dot_tr"], c9 + (i + 1))
                        if i >= 2:
                            act.wait_ge(dot_st[b], h * (16 * (5 - b)) + 16 * (i // 2))
                        for m in range(2):
                            act.activation(o_t[:, b, m, 0:r], ps[:, 7, (2 + m) * P:(2 + m) * P + r], ACT.Copy,
                                           scale=cols[:, 24 + m:25 + m]).then_inc(S["dot_ev"], 1)
                        act.wait_ge(S["dot_ev"], h * (2 * TILES) + 2 * (i + 1))
                        act.dma_start(o_d[bass.ds(h * 2 + 8, 2), :, i * P:i * P + r].rearrange("m p n -> p m n"),
                                      o_t[:, b, :, 0:r]).then_inc(dot_st[b], 16)
                    i = step - 2
                    if 0 <= i < TILES:
                        r, b = rows(i), i % 2
                        keys = P * (i + 1) if i < LAST else NS + PAST
                        act.wait_ge(S["m0_done"], c9 + (i + 1))
                        if i >= 1:
                            act.wait_ge(S["a_done"], c9 + i)
                        act.activation(e0[0:r, 0:keys], s_bank[0:r, 0:keys], ACT.Exp, bias=st[0:r, 24 + b:25 + b],
                                       accum_out=st[0:r, 28 + 2 * b:29 + 2 * b]).then_inc(S["e0_done"], 1)
                    i = step - 1
                    if 0 <= i < TILES:
                        r, b = rows(i), i % 2
                        act.wait_ge(S["d_rope"], h * (2 * TILES) + 2 * (i + 1))
                        out = t["new_k_prompt"][0, 0, i * P:(i + 1) * P] if i < LAST else t["new_k_sample"][0, 0]
                        act.dma_start(out[:, bass.ds(h, 1)].rearrange("t h m d -> t (h m d)"), qk[0:r, b, 2 * P:4 * P]).then_inc(k_st[b], 16)
                    i = step - 2
                    if 0 <= i < TILES:
                        r, b = rows(i), i % 2
                        act.wait_ge(S["m1_done"], c9 + (i + 1))
                        act.activation(e1[0:r, 0:keys], s_bank[0:r, 0:keys], ACT.Exp, bias=st[0:r, 26 + b:27 + b],
                                       accum_out=st[0:r, 29 + 2 * b:30 + 2 * b]).then_inc(S["e1_done"], 1)
                act.wait_ge(S["v_st"], h * (16 * TILES) + 16 * TILES)
                for sems in (k_st, dot_st):
                    act.wait_ge(sems[0], h * (16 * 5) + 16 * 5)
                    act.wait_ge(sems[1], h * (16 * 4) + 16 * 4)

            def load_side(q, src):
                act.dma_start(side(q), src).then_inc(side_in[q % 3], 16)

            def b1_source(q):
                return o_d[q // 2] if q % 2 == 0 else gates_d[q // 2]

            for q in range(3):
                load_side(q, b1_source(q))
            for k in range(KT):
                act.wait_ge(S["pre_done"], 8 + k + 1)
                act.activation(ahi(k), row(1 + k % 2), ACT.Copy).then_inc(S["hi_done"], 1)
                for q in (2 * k + 3, 2 * k + 4):
                    if q < 16:
                        load_side(q, b1_source(q))
            for m in range(8):
                if m >= 3:
                    act.wait_ge(S["acc_free"], A_B1 + m - 2)
                load_side(16 + m, gates_d[8 + m])
            for k in range(3):
                act.wait_ge(S["acc_free"], A_B1 + 6 + k)
                load_side(24 + k, o_d[8 + k])
            act.wait_ge(S["acc_done"], A_B2)
            for k in range(KT):
                act.wait_ge(side_in[(24 + k) % 3], 16 * ((24 + k) // 3 + 1))
                act.activation(ahi(k), side(24 + k), ACT.Copy).then_inc(S["hi_done"], 1)
                act.wait_ge(S["lo_done"], L_B2 + k + 1)
                q = 27 + k
                load_side(q, o_d[8 + k + 3] if q < 32 else gates_d[16 + q - 32])
            for m in range(3, 8):
                act.wait_ge(S["acc_free"], A_B2 + m - 2)
                load_side(32 + m, gates_d[16 + m])
            for m in range(3):
                act.wait_ge(S["acc_free"], A_B2 + 6 + m)
                load_side(40 + m, xt_d[m])
            act.wait_ge(S["acc_done"], A_OUT)
            for k in range(KT):
                act.wait_ge(S["x_add"], k + 1)
                act.activation(ahi(k), x(k), ACT.Copy).then_inc(S["hi_done"], 1)
            for m in range(8):
                act.wait_ge(S["acc_free"], A_OUT + m + 1)
                square(m, 8, SSQ[0])
                if m < 5:
                    load_side(43 + m, xt_d[3 + m])
            act.wait_ge(S["ssq_bc"], 2)
            root_of_mean()
            hi_of_scaled(L_FFN, 16)

            def conv_input(u, n, j, before, free):
                act.wait_ge(S["acc_done"], before)
                act.wait_ge(S["u_free"], free)
                src = acc(n)
                act.copy(u[:, GAP:GAP + 2 * THIRD].rearrange("p (c n) -> p c n", c=2), src[:, 0:2, :])
                act.copy(u[:, GAP + 2 * THIRD:GAP + NP], src[:, 2, 0:NP - 2 * THIRD])
                act.copy(u[:, 2 * GAP + NP:UW], src[:, 2, NP - 2 * THIRD:THIRD]).then_inc(S["acc_free"], 1)

            with act.Fori(0, FT) as j:
                conv_input(u_g, 0, j, j * 2 + (A_UP + 1), j * 2 + 1)
                conv_input(u_v, 1, j, j * 2 + (A_UP + 2), j * 2 + 2)
                act.wait_ge(S["u_free"], j * 2 + 3)
                act.activation(row(1, CW), row(1, CW), ACT.Silu).then_inc(S["silu_done"], 1)
                act.wait_ge(S["hid_done"], j + 2)
                out = hid_d[bass.ds(j, 1)].rearrange("k p n -> p (k n)")
                act.dma_start(out[:, 0:NP], row(5, NP)).then_inc(S["hid_st"], 16)
                act.dma_start(out[:, NP:NT], row(5, CW)[:, NP + GAP:CW]).then_inc(S["hid_st"], 16)
            act.wait_ge(S["hid_st"], 32 * (FT + 1))
            act.wait_ge(S["ul_ev"], 1)
            for w in range(4):
                out = t["conv_prompt" if w < 2 else "conv_sample"][0, 0, w % 2].rearrange("(b j c) -> j b c", b=2, c=P)
                act.dma_start(out, row(1, 2 * P)[w:4 * FT:4, :].rearrange("p (b c) -> p b c", b=2)).then_inc(S["ul_st"], 16)
            act.wait_ge(S["ul_st"], 64)
            with act.Fori(0, 3) as third:
                def load_hidden(g):
                    n = min(3, FT - 3 * g)
                    at = (2 + g % 4) * UW
                    act.dma_start(scr[:, at:at + n * THIRD].rearrange("p (k c) -> p k c", k=n),
                                  hid_d[3 * g:3 * g + n, :, bass.ds(third * THIRD, THIRD)].rearrange("k p n -> p k n")
                                  ).then_inc(hid_in[g % 4], 16)

                for g in range(4):
                    act.wait_ge(S["lo_done"], third * FT + (L_DOWN - FT + min(3 * g + 15, FT)))
                    load_hidden(g)
                act.wait_ge(S["down_free"], third * 8 + 8)
                for k in range(FT):
                    if k % 3 == 0:
                        act.wait_ge(hid_in[k // 3 % 4], third * 32 + 16 * (k // 12 + 1))
                    act.activation(a_hi[:, k * THIRD:(k + 1) * THIRD], hid_piece(k), ACT.Copy).then_inc(S["hi_done"], 1)
                    if k % 3 == 2 and k // 3 < 4:
                        act.wait_ge(S["lo_done"], third * FT + (L_DOWN + k + 1))
                        load_hidden(k // 3 + 4)
                for m in range(8):
                    act.wait_ge(S["down_free"], third * 8 + (9 + m))
                    cut = bass.ds(third * THIRD, THIRD)
                    if m >= 1:
                        act.wait_ge(S["ssq_done"], third * 7 + (SSQ[1] + m - 1))
                    act.activation(row(1, THIRD) if m else row(0)[:, cut], x(m)[:, cut],
                                   ACT.Square).then_inc(S["sq_done"], 1)
            act.wait_ge(S["lo_done"], L_PLE)
            act.dma_start(ple_in[:, 0:LAST, :], t["p_prompt"][0, 0].rearrange("(i p) c -> p i c", p=P)).then_inc(S["ple_in"], 16)
            act.dma_start(ple_in[0:NS, LAST, :], t["p_sample"][0, 0]).then_inc(S["ple_in"], 16)
            act.wait_ge(S["ssq_bc"], 3)
            root_of_mean()
            act.wait_ge(S["down_done"], 24)
            for k in range(KT):
                act.wait_ge(S["pre_done"], 24 + k + 1)
                act.activation(ahi(k), row(1 + k % 2 * 4), ACT.Copy).then_inc(S["hi_done"], 1)
            for b in range(5):
                act.wait_ge(S["ple_tr"], b + 1)
                src, dst = ple_block(b), ple_part(ple_hi, b)
                act.activation(dst, src, ACT.Copy).then_inc(S["ple_hi"], 1)
            for m in range(9):
                if m < 8:
                    act.wait_ge(S["acc_done"], A_PLE + 2 * m + 2)
                    if m:
                        act.wait_ge(S["y_mul"], m)
                    act.activation(thirds(row(0)), acc(1), ACT.Sigmoid).then_inc(S["sig_done"], 1)
                if m:
                    o, b = m - 1, (m - 1) % 2
                    if o >= 2:
                        act.wait_ge(y_st[b], 32 * (o // 2))
                    for part in range(3):
                        act.wait_ge(S["y_tr"], 3 * o + part + 1)
                        if part < 2:
                            act.copy(y_tok[:, b, 4 * part:4 * part + 4, :],
                                     ps[:, 6 + part, :].rearrange("p (i c) -> p i c", c=P)).then_inc(S["y_ev"], 1)
                        else:
                            act.copy(y_tok[0:NS, b, LAST, :], ps[0:NS, 6, 0:P]).then_inc(S["y_ev"], 1)
                    act.wait_ge(S["y_ev"], 3 * m)
                    act.dma_start(t["y_prompt"][0].rearrange("(i p) c -> p i c", p=P)[:, :, o * P:m * P],
                                  y_tok[:, b, 0:LAST, :]).then_inc(y_st[b], 16)
                    act.dma_start(t["y_sample"][0][:, o * P:m * P], y_tok[0:NS, b, LAST, :]).then_inc(y_st[b], 16)
            act.wait_ge(y_st[0], 32 * 4)
            act.wait_ge(y_st[1], 32 * 4)

        @block.vector
        def _(dve):
            dve.memset(ones[:, :], 1.0).then_inc(S["lam_m"], 1)
            dve.memset(eps[:, :], EPS)
            dve.wait_ge(S["vec_in"], 16 * 14)
            dve.tensor_tensor(lamt[:, 4:6], lamt[:, 0:2], lamt[:, 2:4], ALU.mult).then_inc(S["lam_m"], 1)
            dve.wait_ge(S["vec_tr"], 1)
            vp = ps[:, 7, :].rearrange("p (b c) -> p b c", b=4)
            dve.tensor_copy(cols[:, :], vp[:, 0, 0:26]).then_inc(S["vec_ev"], 1)
            dve.tensor_copy(convc[:, :, :].rearrange("p (b w) j -> p b (w j)", b=2), vp[:, 1:3, 0:4 * FT]).then_inc(S["vec_ev"], 1)
            dve.tensor_copy(convs[:, :, :].rearrange("p w j -> p (w j)"), vp[:, 3, 0:4 * FT]).then_inc(S["vec_ev"], 1)
            dve.wait_ge(S["vec_ev"], 3)
            dve.tensor_scalar(cols[:, 24:26], cols[:, 24:26], 1.0 - LAM_INIT, None, ALU.mult).then_inc(S["vec_ev"], 1)
            dve.wait_ge(S["lam_e"], 1)
            dve.scalar_tensor_tensor(lam, lamt[:, 6:7], LAM_INIT, lamt[:, 7:8], ALU.add, ALU.subtract).then_inc(S["lam_d"], 1)
            full_k = full[:, :].rearrange("p (k n) -> p k n", k=KT)
            for i in range(TILES):
                r = rows(i)
                dve.wait_ge(S["x_tr"], i + 1)
                dve.tensor_copy(full_k[:, 4:8, i * P:i * P + r],
                                ps[:, 2 * (i % 2) + 1, :].rearrange("p (k c) -> p k c", k=4)[:, :, 0:r]).then_inc(S["x_ev_d"], 1)

            def add_squares(k, squares, adds):
                dve.wait_ge(S["sq_done"], squares + k + 1)
                if adds + k > 1:
                    dve.wait_ge(S["ssq_done"], adds + k - 1)
                dve.tensor_tensor(row(0), row(0), row(1), ALU.add).then_inc(S["ssq_done"], 1)

            for k in range(1, KT):
                add_squares(k, 0, 0)

            def lo_part(k, src, split0):
                dve.wait_ge(S["hi_done"], split0 + k + 1)
                dve.tensor_tensor(alo(k), src, ahi(k).bitcast(F32), ALU.subtract).then_inc(S["lo_done"], 1)

            def norm_and_split(g, split0, norms, pre0, far=1):
                dve.wait_ge(S["rms_rt"], norms)
                dve.reciprocal(row(0), row(0)).then_inc(S["rms_inv"], 1)
                dve.wait_ge(S["rms_inv"], norms)
                for k in range(KT + 1):
                    if k < KT:
                        if k >= 2:
                            dve.wait_ge(S["lo_done"], split0 + k - 1)
                        dve.scalar_tensor_tensor(row(1 + k % 2 * far), x(k), cols[:, g + k:g + k + 1], row(0),
                                                 ALU.mult, ALU.mult).then_inc(S["pre_done"], 1)
                    if k:
                        lo_part(k - 1, row(1 + (k - 1) % 2 * far), split0)

            norm_and_split(0, L_MIX, 1, 0)

            dve.wait_ge(S["head_const"], 5 * 16)
            dve.tensor_scalar(gqk[:, 0, :], gqk[:, 0, :], DK ** -0.5, None, ALU.mult).then_inc(S["g_scaled"], 1)

            def rotate(src, i, groups, prods, before_p, before_o, done, in_place):
                r, ti = rows(i), i if i < LAST else PAST // P
                a = nrm[0:r, 0:groups * P].rearrange("p (g s c) -> p g s c", g=groups, s=2)
                bb = rope_b[0:r, 0:groups * P].rearrange("p (g s c) -> p g s c", g=groups, s=2)
                x4 = src.rearrange("p (g s c) -> p g s c", g=groups, s=2)
                sn = bcast(sin[0:r, ti, :], groups)
                dve.tensor_tensor(bb[:, :, 0, :], x4[:, :, 1, :], sn, ALU.mult).then_inc(prods, 1)
                dve.tensor_tensor(bb[:, :, 1, :], x4[:, :, 0, :], sn, ALU.mult).then_inc(prods, 1)
                if in_place:
                    dve.wait_ge(prods, before_p + 2)
                dve.tensor_tensor(a.rearrange("p g s c -> p (g s) c"), src.rearrange("p (g c) -> p g c", c=DK // 2),
                                  bcast(cos[0:r, ti, :], 2 * groups), ALU.mult).then_inc(prods, 1)
                dve.wait_ge(prods, before_p + 3)
                out = qk[0:r, i % 2, 0:groups * P].rearrange("p (g s c) -> p g s c", g=groups, s=2)
                dve.tensor_tensor(out[:, :, 0, :], a[:, :, 0, :], bb[:, :, 0, :], ALU.subtract).then_inc(done, 1)
                dve.tensor_tensor(out[:, :, 1, :], a[:, :, 1, :], bb[:, :, 1, :], ALU.add).then_inc(done, 1)

            with dve.Fori(0, HEADS) as h:
                c9 = h * TILES
                dve.wait_ge(S["head_in"], h * 32 + 32)
                for step in range(TILES + 3):
                    i = step
                    if i < TILES:
                        r = rows(i)
                        dve.wait_ge(S["v_done"], c9 + (i + 1))
                        if i >= 1:
                            dve.wait_ge(S["rope_done"], h * (2 * TILES) + 2 * i)
                        if i >= 2:
                            dve.wait_ge(S["qk_tr"], c9 + (i - 1))
                            dve.wait_ge(S["kd_done"], c9 + (i - 1))
                        rotate(ps[0:r, i % 3, 0:2 * P], i, 2, S["rope_m"], h * (3 * TILES) + 3 * i, None,
                               S["rope_done"], False)
                        dve.wait_ge(S["rope_done"], h * (2 * TILES) + 2 * (i + 1))
                        if i >= 3:
                            dve.wait_ge(S["kv_done"], c9 + (i - 2))
                        c = 2 * P + (i == LAST)
                        dve.tensor_scalar(kd[0:r, i % 3, :], qk[0:r, i % 2, P:2 * P], hc[0:r, c:c + 1], None,
                                          ALU.mult).then_inc(S["kd_done"], 1)
                    i = step - 1
                    if 0 <= i < TILES:
                        r = rows(i)
                        dve.wait_ge(S["qk_ev"], c9 + (i + 1))
                        if i >= 2:
                            dve.wait_ge(S["o_done"], c9 + (i - 1))
                        dve.tensor_tensor(q_d[:, i % 2, 0:r], qk_t[:, i % 2, 0:r], hc[:, P:P + r],
                                          ALU.mult).then_inc(S["qd_done"], 1)
                    i = step - 2
                    if 0 <= i < TILES:
                        r = rows(i)
                        dve.wait_ge(S["sc_done"], c9 + (i + 1))
                        dve.tensor_tensor(s_m[0:r, i % 2, 0:r], ps[0:r, 5, 0:r], hc[0:r, 0:r],
                                          ALU.mult).then_inc(S["sm_done"], 1)
                    i = step - 3
                    if 0 <= i < TILES:
                        r, b = rows(i), i % 2
                        dve.wait_ge(S["kv_done"], c9 + (i + 1))
                        if i == 0:
                            dve.tensor_copy(s_p, ps[:, 7, 0:DV]).then_inc(S["state_done"], 1)
                        else:
                            s_x, c = (s_p, 2 * P + 2) if i < LAST else (s_s, 2 * P + 3)
                            dve.wait_ge(S["state_done"], c9 + i)
                            dve.scalar_tensor_tensor(s_x, s_x, hc[:, c:c + 1], ps[:, 7, 0:DV],
                                                     ALU.mult, ALU.add).then_inc(S["state_done"], 1)
                        dve.wait_ge(S["o_rt"], c9 + (i + 1))
                        dve.reciprocal(st[0:r, 4 + b:5 + b], st[0:r, 2 + b:3 + b]).then_inc(S["o_inv"], 1)
                dve.wait_ge(S["ot_ev"], c9 + TILES)

            dve.wait_ge(S["g_scaled"], 1)
            with dve.Fori(0, HEADS) as h:
                c9 = h * TILES
                dve.wait_ge(S["dc_tr"], h + 1)
                dve.tensor_copy(k_t[:, :, NT:NT + PAST],
                                ps[:, 4, 0:2 * P].rearrange("p (m n) -> p m n", m=2)).then_inc(S["dc_ev"], 1)
                for step in range(DIFF_STEPS):
                    i = step - 4
                    if 0 <= i < TILES:
                        r, b = rows(i), i % 2
                        dve.wait_ge(S["do_rt"], c9 + (i + 1))
                        dve.reciprocal(st[0:r, 4 + b:5 + b], st[0:r, 2 + b:3 + b]).then_inc(S["do_inv"], 1)
                    i = step - 2
                    if 0 <= i < TILES:
                        r, b = rows(i), i % 2
                        keys = P * (i + 1) if i < LAST else NS + PAST
                        dve.wait_ge(S["s0_done"], c9 + (i + 1))
                        dve.tensor_reduce(st[0:r, 24 + b:25 + b], s_bank[0:r, 0:keys], axis=AX_X, op=ALU.max,
                                          negate=True).then_inc(S["m0_done"], 1)
                    i = step - 3
                    if 0 <= i < TILES:
                        r, n = rows(i), min(4, i + 1) if i < LAST else 2
                        dve.wait_ge(S["at0_tr"], c9 + (i + 1))
                        if i >= 1:
                            dve.wait_ge(S["pv_done"], c9 + i)
                        dve.tensor_copy(a_t[:, 0:n, 0:r],
                                        ps[:, 4, :].rearrange("p (b n) -> p b n", b=4)[:, 0:n, 0:r]).then_inc(S["at0_ev"], 1)
                    i = step - 1
                    if 0 <= i < TILES:
                        r, b = rows(i), i % 2
                        dve.wait_ge(S["d_rt"], c9 + (i + 1))
                        dve.reciprocal(st[0:r, 36 + 4 * b:40 + 4 * b], st[0:r, 16 + 4 * b:20 + 4 * b]).then_inc(S["d_inv"], 1)
                        dve.wait_ge(S["d_inv"], c9 + (i + 1))
                        for m in range(4):
                            bank, at = (2 * b, m * P) if m < 3 else (2 * b + 1, 0)
                            if m == 3:
                                dve.wait_ge(S["d_v"], c9 + (i + 1))
                            dve.scalar_tensor_tensor(nrm[0:r, m * P:(m + 1) * P], ps[0:r, bank, at:at + P],
                                                     st[0:r, 36 + 4 * b + m:37 + 4 * b + m], gqk[0:r, m // 2, :],
                                                     ALU.mult, ALU.mult).then_inc(S["d_nrm"], 1)
                        dve.wait_ge(S["d_nrm"], h * (4 * TILES) + 4 * (i + 1))
                        if i >= 2:
                            dve.wait_ge(S["d_tr"], c9 + (i - 1))
                            dve.wait_ge(k_st[b], h * (16 * (5 - b)) + 16 * (i // 2))
                        rotate(nrm[0:r, :], i, 4, S["d_ropem"], h * (3 * TILES) + 3 * i, None, S["d_rope"], True)
                    i = step - 2
                    if 0 <= i < TILES:
                        r, b = rows(i), i % 2
                        dve.wait_ge(S["s1_done"], c9 + (i + 1))
                        dve.tensor_reduce(st[0:r, 26 + b:27 + b], s_bank[0:r, 0:keys], axis=AX_X, op=ALU.max,
                                          negate=True).then_inc(S["m1_done"], 1)
                    i = step - 3
                    if 4 <= i < LAST:
                        dve.wait_ge(S["at1_tr"], h * 4 + (i - 3))
                        dve.tensor_copy(a_t[:, 4:i + 1, :],
                                        ps[:, 4, 0:(i - 3) * P].rearrange("p (b n) -> p b n", n=P)).then_inc(S["at1_ev"], 1)
                    i = step - 2
                    if 0 <= i < TILES:
                        r, b = rows(i), i % 2
                        dve.wait_ge(S["e1_done"], c9 + (i + 1))
                        dve.reciprocal(st[0:r, 32 + 2 * b:34 + 2 * b], st[0:r, 28 + 2 * b:30 + 2 * b]).then_inc(S["r_inv"], 1)
                        dve.wait_ge(S["r_inv"], c9 + (i + 1))
                        r1 = st[0:r, 33 + 2 * b:34 + 2 * b]
                        dve.tensor_tensor(r1, r1, lam[0:r, :], ALU.mult).then_inc(S["r_lam"], 1)
                        dve.wait_ge(S["r_lam"], c9 + (i + 1))
                        dve.tensor_scalar(e1[0:r, 0:keys], e1[0:r, 0:keys], r1, None, ALU.mult).then_inc(S["t_done"], 1)
                        dve.wait_ge(S["t_done"], c9 + (i + 1))
                        if i >= 1:
                            dve.wait_ge(S["at0_tr"], c9 + i)
                        if 4 <= i - 1 < LAST:
                            dve.wait_ge(S["at1_tr"], h * 4 + (i - 4))
                        dve.scalar_tensor_tensor(a_w[0:r, 0:keys], e0[0:r, 0:keys], st[0:r, 32 + 2 * b:33 + 2 * b],
                                                 e1[0:r, 0:keys], ALU.mult, ALU.subtract).then_inc(S["a_done"], 1)
                    i = step - 1
                    if 0 <= i < TILES:
                        r, b = rows(i), i % 2
                        dve.wait_ge(S["d_tr"], c9 + (i + 1))
                        if i >= 2:
                            dve.wait_ge(S["s1_done"], c9 + (i - 1))
                        v4 = ps[:, 4, :].rearrange("p (m n) -> p m n", m=4)
                        dve.tensor_copy(q_t[:, b, :, 0:r], v4[:, 0:2, 0:r]).then_inc(S["d_ev"], 1)
                        dve.tensor_copy(k_t[:, :, i * P:i * P + r], v4[:, 2:4, 0:r]).then_inc(S["d_ev"], 1)
                dve.wait_ge(S["dot_ev"], h * (2 * TILES) + 2 * TILES)

            for k in range(KT + 1):
                if k < KT:
                    for q in (2 * k, 2 * k + 1):
                        dve.wait_ge(side_in[q % 3], 16 * (q // 3 + 1))
                    if k >= 2:
                        dve.wait_ge(S["lo_done"], L_B1 + k - 1)
                    dve.tensor_tensor(row(1 + k % 2), side(2 * k), side(2 * k + 1), ALU.mult).then_inc(S["pre_done"], 1)
                if k:
                    lo_part(k - 1, row(1 + (k - 1) % 2), L_B1)
            for m in range(8):
                q = 16 + m
                dve.wait_ge(side_in[q % 3], 16 * (q // 3 + 1))
                dve.wait_ge(S["acc_done"], A_B1 + m + 1)
                dve.tensor_tensor(thirds(x(m)), acc(m), thirds(side(q)), ALU.mult).then_inc(S["acc_free"], 1)
            for k in range(KT):
                lo_part(k, side(24 + k), L_B2)
            for m in range(8):
                q = 32 + m
                dve.wait_ge(side_in[q % 3], 16 * (q // 3 + 1))
                dve.wait_ge(S["acc_done"], A_B2 + m + 1)
                if m >= 2:
                    dve.wait_ge(S["x_add"], m - 1)
                else:
                    dve.wait_ge(S["lo_done"], L_B1 + KT)
                dve.tensor_tensor(thirds(row(1 + m % 2)), acc(m), thirds(side(q)), ALU.mult).then_inc(S["acc_free"], 1)
                dve.wait_ge(S["acc_free"], A_B2 + m + 1)
                dve.tensor_tensor(x(m), x(m), row(1 + m % 2), ALU.add).then_inc(S["x_add"], 1)
            dve.wait_ge(S["x_add"], 8)
            for k in range(KT):
                lo_part(k, x(k), L_OUT)
            dve.wait_ge(S["lo_done"], L_OUT + KT)
            for m in range(9):
                if m < 8:
                    q = 40 + m
                    dve.wait_ge(side_in[q % 3], 16 * (q // 3 + 1))
                    dve.wait_ge(S["acc_done"], A_OUT + m + 1)
                    dve.tensor_tensor(thirds(x(m)), acc(m), thirds(side(q)), ALU.add).then_inc(S["acc_free"], 1)
                if m >= 2:
                    add_squares(m - 1, 8, SSQ[0])
            norm_and_split(8, L_FFN, 2, 16)

            dve.wait_ge(S["acc_free"], A_UP)
            dve.wait_ge(S["lo_done"], L_DOWN)
            dve.memset(u_g[:, 0:GAP], 0.0).then_inc(S["u_free"], 1)
            dve.memset(u_v[:, 0:GAP], 0.0).then_inc(S["u_free"], 1)
            dve.memset(row(5, 2), 0.0).then_inc(S["hid_done"], 1)
            dve.wait_ge(S["hid_done"], 1)
            dve.memset(row(5, 2), 0.0).then_inc(S["hid_st"], 32)
            with dve.Fori(0, FT) as j:
                for half, (u, c) in enumerate(((u_g, row(1, CW)), (u_v, row(2, CW)))):
                    def col(w):
                        return convc[:, w, bass.ds(j + half * FT, 1)]

                    dve.wait_ge(S["u_free"], j * 2 + (half + 1))
                    dve.tensor_copy(u[:, GAP + NP:2 * GAP + NP], convs[:, :, bass.ds(j + half * FT, 1)].rearrange("p w a -> p (w a)")).then_inc(S["u_pad"], 1)
                    dve.wait_ge(S["acc_free"], j * 2 + (A_UP + half + 1))
                    at = (3 + half) * UW + NP
                    ends = scr[:, at:at + 2 * (NS + GAP)].rearrange("p (a b) -> p a b", a=2)[:, :, 0:GAP]
                    dve.tensor_copy(u_last[:, bass.ds(j + half * FT, 1), :].rearrange("p a (s w) -> p (a s) w", w=GAP),
                                    ends).then_inc(S["u_last_done"], 1)
                    dve.wait_ge(S["u_pad"], j * 2 + (half + 1))
                    dve.wait_ge(S["hid_done"], j + 1)
                    dve.tensor_scalar(c, u[:, 2:2 + CW], col(2), col(3), ALU.mult, ALU.add).then_inc(S["conv_t"], 1)
                    dve.wait_ge(S["conv_t"], j * 4 + (2 * half + 1))
                    dve.scalar_tensor_tensor(c, u[:, 1:1 + CW], col(1), c, ALU.mult, ALU.add).then_inc(S["conv_t"], 1)
                    dve.wait_ge(S["conv_t"], j * 4 + (2 * half + 2))
                    dve.scalar_tensor_tensor(c, u[:, 0:CW], col(0), c, ALU.mult, ALU.add).then_inc(S["u_free"], 1)
                dve.wait_ge(S["silu_done"], j + 1)
                dve.wait_ge(S["u_free"], j * 2 + 4)
                dve.wait_ge(S["hid_st"], j * 32 + 32)
                dve.tensor_tensor(row(5, CW), row(1, CW), row(2, CW), ALU.mult).then_inc(S["hid_done"], 1)
            dve.wait_ge(S["ul_tr"], 1)
            dve.wait_ge(S["hid_done"], FT + 1)
            dve.tensor_copy(row(1, 2 * P)[0:4 * FT, :], ps[0:4 * FT, 7, 0:2 * P]).then_inc(S["ul_ev"], 1)
            dve.wait_ge(S["acc_free"], A_PLE)
            dve.wait_ge(S["ul_ev"], 1)
            dve.memset(lamt[:, 0:1], 0.0).then_inc(S["down_free"], 8)

            with dve.Fori(0, 3) as third:
                for k in range(FT):
                    cut = slice(k * THIRD, (k + 1) * THIRD)
                    dve.wait_ge(S["hi_done"], third * FT + (L_DOWN + k + 1))
                    dve.tensor_tensor(a_lo[:, cut], hid_piece(k), a_hi[:, cut].bitcast(F32),
                                      ALU.subtract).then_inc(S["lo_done"], 1)
                cut = bass.ds(third * THIRD, THIRD)
                for m in range(9):
                    if m < 8:
                        dve.wait_ge(S["down_done"], third * 8 + (m + 1))
                        dve.tensor_tensor(x(m)[:, cut], x(m)[:, cut], ps[:, m, 0:THIRD], ALU.add).then_inc(S["down_free"], 1)
                    if m >= 2:
                        dve.wait_ge(S["sq_done"], third * 8 + (16 + m))
                        dve.wait_ge(S["ssq_done"], third * 7 + (SSQ[1] + m - 2))
                        dve.tensor_tensor(row(0)[:, cut], row(0)[:, cut], row(1, THIRD), ALU.add).then_inc(S["ssq_done"], 1)
            norm_and_split(16, L_PLE, 3, 24, far=4)
            for b in range(5):
                dve.wait_ge(S["ple_hi"], b + 1)
                dve.tensor_tensor(ple_part(ple_lo, b), ple_block(b), ple_part(ple_hi, b).bitcast(F32),
                                  ALU.subtract).then_inc(S["ple_lo"], 1)
            for m in range(8):
                dve.wait_ge(S["sig_done"], m + 1)
                if m:
                    dve.wait_ge(S["y_done"], m)
                dve.tensor_tensor(thirds(row(1)), acc(0), thirds(row(0)), ALU.mult).then_inc(S["y_mul"], 1)
                dve.wait_ge(S["y_mul"], m + 1)
                dve.tensor_tensor(x(m), x(m), row(1), ALU.add).then_inc(S["y_done"], 1)


INPUTS = ["x_prompt", "x_sample", "cache_k", "cache_v", "state_ret", "state_conv", "p_prompt", "p_sample",
          "g_mix", "w_in", "g_qn", "g_kn", "lam_q1", "lam_k1", "lam_q2", "lam_k2", "g_dnorm", "w_ret_br",
          "w_da_br", "w_out", "g_ffn", "w_up", "conv_w", "conv_b", "w_down", "g_ple", "w_ple_gate", "w_ple"]
OUTPUTS = [("y_prompt", (1, NP, D)), ("y_sample", (1, NS, D)),
           ("new_k_prompt", (1, 1, NP, HEADS, 2, DK)), ("new_k_sample", (1, 1, NS, HEADS, 2, DK)),
           ("new_v_prompt", (1, 1, NP, HEADS, DV)), ("new_v_sample", (1, 1, NS, HEADS, DV)),
           ("ret_prompt", (1, 1, HEADS, DK, DV)), ("ret_sample", (1, 1, HEADS, DK, DV)),
           ("conv_prompt", (1, 1, 2, 2 * FF)), ("conv_sample", (1, 1, 2, 2 * FF))]


def shape_constants():
    import numpy as np
    inv = np.float32(10000.0) ** (-np.arange(0, DK, 2, dtype=np.float32) / np.float32(DK))
    ang = np.arange(NP, dtype=np.float32)[:, None] * inv[None, :].astype(np.float32)
    ang = ang.reshape(NP // P, P, DK // 2).transpose(1, 0, 2)
    idx = np.arange(P, dtype=np.float64)
    ret = np.zeros((HEADS, P, HC))
    for h in range(HEADS):
        log_g = np.log(1.0 - 2.0 ** (-5.0 - h))
        diff = idx[None, :] - idx[:, None]
        ret[h, :, 0:P] = np.where(diff >= 0, np.exp(log_g * np.maximum(diff, 0)), 0.0) * DK ** -0.5
        ret[h, :, P:2 * P] = np.exp((idx + 1) * log_g)[None, :]
        ret[h, :, 2 * P] = np.exp((P - 1 - idx) * log_g) * DK ** -0.5
        ret[h, :, 2 * P + 1] = np.exp((NS - 1 - idx) * log_g) * DK ** -0.5
        ret[h, :, 2 * P + 2] = np.exp(P * log_g)
        ret[h, :, 2 * P + 3] = np.exp(NS * log_g)
    mask = np.zeros((1, 2 * P))
    mask[0, 0:P // 2] = 1.0
    mask[0, P + P // 2:] = MASKED
    out = {"c_cos": np.cos(ang), "c_sin": np.sin(ang), "c_ret": ret, "c_mask": mask, "c_ident": np.eye(P)}
    return {k: np.ascontiguousarray(v.astype(np.float32)) for k, v in out.items()}


def kernel(**inputs):
    import numpy as np
    import concourse.bacc as bacc
    from concourse.bass_utils import run_bass_kernel_spmd

    nc = bacc.Bacc("TRN2", target_bir_lowering=False, num_devices=1)
    arrays = {n: np.ascontiguousarray(inputs[n]) for n in INPUTS}
    arrays.update(shape_constants())
    t = {n: nc.dram_tensor(n, a.shape, F32, kind="ExternalInput").ap() for n, a in arrays.items()}
    for n, shape in OUTPUTS:
        t[n] = nc.dram_tensor(n, shape, F32, kind="ExternalOutput").ap()
    kernel_program(nc, t)
    r = run_bass_kernel_spmd(nc, [arrays], core_ids=[0])
    return tuple(r.results[0][n] for n, _ in OUTPUTS)
```

```python
import math
from contextlib import ExitStack

import concourse.bass as bass
from concourse import mybir

F32 = mybir.dt.float32
F32R = mybir.dt.float32r
ALU = mybir.AluOpType
ACT = mybir.ActivationFunctionType
AX_X = mybir.AxisListType.X

P = 128
D = 1024
KT = D // P
NP = 1024
NS = 32
NT = NP + NS
PAST = 128
TILES = NP // P + 1
LAST = TILES - 1
THIRD = NT // 3
HEADS = 4
DK, DV = 128, 256
FF = 2816
FT = FF // P
GAP = 2
UW = NT + 2 * GAP
CW = UW - GAP
EPS = 1e-6
LAM_INIT = 0.8 - 0.6 * math.exp(-0.3 * 0)
MASKED = -1e30
SLOTS = 8
RAW = 4
C_RQ, C_RK, C_RV, C_RG, C_DQ, C_DK, C_DV, C_GA = 0, 512, 1024, 2048, 3072, 4096, 5120, 6144
GATES = 24
FIRST = 12
U_RET = FIRST
U_DIFF = U_RET + 5 * HEADS
U_B = U_DIFF + 8 * HEADS
U_UP = U_B + 24
U_DOWN = U_UP + 2 * FT
U_PLE = U_DOWN + 3 * 24
U_PG = U_PLE + 2
A_DIFF = FIRST + HEADS
A_B1, A_B2, A_OUT, A_UP = GATES, GATES + 8, GATES + 16, GATES + 24
A_PLE = A_UP + 2 * FT
DIFF_STEPS = TILES + 5
EARLY = 3
RET_GATE_SLOT, DIFF_GATE_SLOT = 3, 6
L_B1 = TILES
L_B2, L_OUT, L_FFN = L_B1 + 8, L_B1 + 16, L_B1 + 24
H_DOWN = L_FFN + 24
H_PLE = H_DOWN + 3 * FT


def on_pool(norm, n):
    return n % 2 == 1 if norm == 0 else n % 6 != 0


def pieces_before(norm, n, pool):
    return sum(on_pool(norm, i) == pool for i in range(n))


L_DOWN = L_FFN + pieces_before(0, 24, False)
L_PLE = L_DOWN + 3 * FT
PRE_FFN, PRE_PLE = TILES, TILES + 24
USED_B1, USED_B2, USED_UP = 0, 7, 14
PG_SLOTS = (6, 7, 3)
HID_GROUPS = (0, 3, 7, 11, 16, FT)
Q_A, Q_GA, Q_B, Q_GB, Q_X = 0, 8, 16, 24, 32
SSQ_DOWN = 9
HC = 2 * P + 4


def rows(i):
    return P if i < LAST else NS


def kernel_program(nc, t):
    with ExitStack() as ctx:
        def sb(name, shape, dt=F32):
            return ctx.enter_context(nc.sbuf_tensor(name, shape, dt))

        def sem(name):
            return ctx.enter_context(nc.semaphore(name))

        def dram(name, shape):
            return nc.dram_tensor(name, shape, F32, kind="Internal").ap()

        w_raw = sb("w_raw", [P, RAW, 8 * P])
        w_hi = sb("w_hi", [P, SLOTS, 8 * P], F32R)
        w_lo = sb("w_lo", [P, SLOTS, 8 * P], F32R)
        a_hi = sb("a_hi", [P, KT * NT], F32R)
        a_lo_at = -(-nc.sbuf_base // 32) * 32
        a_lo = sb("a_lo", [P, KT * NT], F32R)
        a_pre = nc.alloc_sbuf_tensor_at("a_pre", [P, KT * NT], F32, offset=a_lo_at)
        full = sb("full", [P, KT * NT])
        scr = sb("scr", [P, 6 * UW])
        ident = sb("ident", [P, P])
        ones = sb("ones", [P, P])
        cols = sb("cols", [P, 26])
        convc = sb("convc", [P, 4, 2 * FT])
        convs = sb("convs", [P, 2, 2 * FT])
        u_last = sb("u_last", [P, 2 * FT, 4])
        lamt = sb("lamt", [P, 9])
        eps = sb("eps", [P, 1])
        ps = ctx.enter_context(nc.psum_tensor("ps", [P, 8, 512], F32))

        gates_d = dram("gates_d", [GATES, P, NT])
        o_d = dram("o_d", [16, P, NT])
        xt_d = dram("xt_d", [KT, P, NT])
        hid_d = dram("hid_d", [FT, P, NT])

        def ahi(k):
            return a_hi[:, k * NT:(k + 1) * NT]

        def alo(k):
            return a_lo[:, k * NT:(k + 1) * NT]

        def apre(k):
            return a_pre[:, k * NT:(k + 1) * NT]

        def x(k):
            return full[:, k * NT:(k + 1) * NT]

        def row(j, n=NT):
            return scr[:, j * UW:j * UW + n]

        def thirds(v):
            return v.rearrange("p (c n) -> p c n", c=3)

        def acc(n):
            b = 3 * (n % 2)
            return ps[:, b:b + 3, 0:THIRD]

        def wk(w, slot, k):
            return w[:, slot, k * P:(k + 1) * P]

        xin = scr[:, 0:3 * D].rearrange("p (b n) -> p b n", b=3)
        vecs = scr[:, 3 * D:3 * D + 4 * P].rearrange("p (b n) -> p b n", b=4)
        xn = scr[:, 3 * D + 4 * P:5 * D + 4 * P].rearrange("p (b n) -> p b n", b=2)
        a_pre_k = a_pre[:, :].rearrange("p (k n) -> p k n", k=KT)
        a_lo_k = a_lo[:, :].rearrange("p (k n) -> p k n", k=KT)
        a_hi_k = a_hi[:, :].rearrange("p (k n) -> p k n", k=KT)

        class Carve:
            def __init__(self, tensor, words):
                self.tensor, self.words, self.at = tensor, words, 0

            def take(self, n):
                self.at += n
                assert self.at <= self.words
                return self.tensor[:, self.at - n:self.at]

        f, s = Carve(full, KT * NT), Carve(scr, 6 * UW)
        cos = f.take(8 * 64).rearrange("p (t c) -> p t c", t=8)
        sin = f.take(8 * 64).rearrange("p (t c) -> p t c", t=8)
        gqk = f.take(2 * P).rearrange("p (g c) -> p g c", g=2)
        mask = f.take(2 * P)
        k_t_at = f.at
        k_t = f.take(2 * (NT + PAST)).rearrange("p (m n) -> p m n", m=2)
        v_tok = f.take((TILES + 1) * DV).rearrange("p (t c) -> p t c", t=TILES + 1)
        nrm_at = f.at
        nrm = f.take(512)
        a_t = f.take(1024).rearrange("p (b n) -> p b n", b=8)
        kc = f.take(2 * P)
        rope_b = s.take(512)
        qk = s.take(2 * 512).rearrange("p (b n) -> p b n", b=2)
        e0 = s.take(1024)
        e1 = s.take(1024)
        a_w = s.take(1024)
        q_t = s.take(2 * 2 * P).rearrange("p (b m n) -> p b m n", b=2, m=2)
        o_n = s.take(2 * DV).rearrange("p (b n) -> p b n", b=2)
        o_t = s.take(2 * DV).rearrange("p (b m n) -> p b m n", b=2, m=2)
        st = s.take(48)
        at = nrm_at + 256
        gates_h = (scr[:, 3616:3616 + NT], full[:, at:at + NT])
        hc = full[:, at + NT:at + NT + HC]
        kd = k_t[:, 0, 0:3 * P].rearrange("p (b n) -> p b n", b=3)
        s_m = k_t[:, 0, 384:640].rearrange("p (b n) -> p b n", b=2)
        qk_t = k_t[:, 1, 0:512].rearrange("p (b n) -> p b n", b=2)
        q_d = k_t[:, 1, 512:768].rearrange("p (b n) -> p b n", b=2)
        gate_row = scr[:, 512 + 2 * 512 + 1024:512 + 2 * 512 + 1024 + NT]
        s_p, s_s = e0[:, 0:DV], e0[:, DV:2 * DV]

        names = """const_in gain_in vec_in xt_st gain_tr gain_ev vec_tr vec_ev lam_m lam_s lam_e lam_d
            x_tr x_ev_a x_ev_d xs_done xr_done xi_done xn_done xn_tr tail_x gate_part gate_ev gate_sig a_used hid_used sq_done ssq_done ssq_bc rms_rt rms_inv g_scaled
            w_begun tail_begun pre_done hi_done lo_done lo_pool w_hi_done down_hi w_split acc_done acc_free 
            head_const head_in ret_proj rope_m rope_done kd_done v_done qk_tr qk_ev qd_done
            sc_done sm_done o_done kv_done state_done o_sq o_rt o_inv o_nrm ot_tr ot_ev s_out
            d_in dc_tr dc_ev pa_done pb_done d_sq d_rt d_inv d_nrm d_ropem d_rope d_v d_tr d_ev
            s0_done s1_done m0_done m1_done e0_done e1_done r_inv r_lam t_done a_done
            at0_tr at1_tr at0_ev at1_ev pv_done do_sq do_rt do_inv do_nrm dot_tr dot_ev v_st
            x_add u_pad u_free conv_t silu_done hid_done hid_st u_last_done
            down_done down_free ul_tr ul_ev ul_st ple_in ple_tr ple_hi ple_lo
            sig_done y_mul y_done y_tr y_ev"""
        S = {n: sem(n) for n in names.split()}
        part_st = [sem(f"part_st{j}") for j in range(2)]
        w_landed = [sem(f"w_landed{j}") for j in range(RAW)]
        x_landed = [sem(f"x_landed{j}") for j in range(3)]
        side_in = [sem(f"side_in{j}") for j in range(3)]
        hid_in = [sem(f"hid_in{j}") for j in range(len(HID_GROUPS) - 1)]
        gate_st = [sem(f"gate_st{j}") for j in range(2)]
        ot_st = [sem(f"ot_st{j}") for j in range(2)]
        dot_st = [sem(f"dot_st{j}") for j in range(2)]
        k_st = [sem(f"k_st{j}") for j in range(2)]
        y_st = [sem(f"y_st{j}") for j in range(2)]

        w_in = t["w_in"][0].rearrange("(k p) n -> p k n", p=P)
        w_of = {n: t[n][0].rearrange("(k p) n -> p k n", p=P)
                for n in ("w_ret_br", "w_da_br", "w_out", "w_up", "w_down", "w_ple_gate", "w_ple")}
        lam = lamt[:, 8:9]

        def bcast(v, n):
            return v.unsqueeze(1).broadcast_to([v.shape[0], n, v.shape[1]])

        def gate_piece(n):
            return (rope_b, nrm)[n % 2][:, 0:THIRD]

        def wait_piece(eng, h, n, whole, part):
            if n % 3 == 2:
                eng.wait_ge(whole, h * 2 + (A_DIFF + n // 3 + 1))
            else:
                eng.wait_ge(part, h * 4 + (2 * HEADS + 2 * (n // 3) + n % 3 + 1))

        def side(q):
            return row(3 + q % 3) if q >= 4 else full[:, k_t_at + q * NT:k_t_at + (q + 1) * NT]

        def down_words(j):
            return 8 * P if j % 3 < 2 else (FT - 16) * P

        def third_of(v, c):
            return v[:, c * THIRD:(c + 1) * THIRD]

        def hid_group(g):
            return HID_GROUPS[g], HID_GROUPS[g + 1]

        def load_hidden(eng, g, third):
            k0, k1 = hid_group(g)
            eng.dma_start(a_pre[:, k0 * THIRD:k1 * THIRD].rearrange("p (k c) -> p k c", c=THIRD),
                          hid_d[k0:k1, :, bass.ds(third * THIRD, THIRD)].rearrange("k p n -> p k n")
                          ).then_inc(hid_in[g], 16)

        ple_in = scr[:, 2 * UW:2 * UW + TILES * 2 * P].rearrange("p (i c) -> p i c", i=TILES)
        ple_hi = w_hi[:, 0:3, :].rearrange("p s c -> p (s c)")[:, 0:2 * NT]
        ple_lo = w_lo[:, 0:3, :].rearrange("p s c -> p (s c)")[:, 0:2 * NT]
        ul_rows = scr[:, 2 * UW + TILES * 2 * P:2 * UW + TILES * 2 * P + 2 * P]
        y_tok = scr[:, 2 * UW:2 * UW + 2 * TILES * P].rearrange("p (b i c) -> p b i c", b=2, i=TILES)
        s_bank = ps[:, 5:7, :].rearrange("p b n -> p (b n)")

        def ple_part(v, b):
            n = 2 * P if b < 4 else NS
            return v.rearrange("p (k n) -> p k n", k=2)[:, :, 2 * b * P:2 * b * P + n]

        def ple_block(b):
            n = 2 * P if b < 4 else NS
            return ps[:, 6 + b % 2, :].rearrange("p (k n) -> p k n", k=2)[:, :, 0:n]

        u_g, u_v = scr[:, 3 * UW:4 * UW], scr[:, 4 * UW:5 * UW]

        block = ctx.enter_context(nc.Block())

        @block.sync
        def _(sp):
            def load_x(i):
                if i >= 3:
                    sp.wait_ge(S["x_tr"], i - 2)
                    sp.wait_ge(S["xn_done"], i - 2)
                src = t["x_prompt"][0, i * P:(i + 1) * P, :] if i < LAST else t["x_sample"][0]
                sp.dma_start(xin[0:rows(i), i % 3, :], src).then_inc(x_landed[i % 3], 16)

            def weights(before, j, src, wait=True):
                if wait:
                    sp.wait_ge(S["w_split"], before + (j - 3))
                dst = w_raw[:, j % RAW, 0:src.shape[1] * src.shape[2]]
                sp.dma_start(dst.rearrange("p (k c) -> p k c", k=src.shape[1]), src).then_inc(w_landed[j % RAW], 16)

            def first_weights(j):
                weights(0, j, w_in[:, :, C_RG + j * P:C_RG + (j + 1) * P], wait=False)

            load_x(0)
            sp.dma_start(ident[:, :], t["c_ident"]).then_inc(S["const_in"], 16)
            for at, n, name in ((0, 8, "g_mix"), (8, 8, "g_ffn"), (16, 8, "g_ple"), (24, 2, "g_dnorm")):
                sp.dma_start(vecs[at:at + n, 0, :], t[name][0].rearrange("(r c) -> r c", c=P)).then_inc(S["gain_in"], 16)
            load_x(1)
            first_weights(0)
            load_x(2)
            for i in range(3, TILES):
                load_x(i)
                if i % 2 == 0 and i // 2 - 1 < RAW:
                    first_weights(i // 2 - 1)
            taps = t["conv_w"][0].rearrange("w (j c) -> w j c", c=P)
            for w in range(3):
                sp.dma_start(vecs[44 * (w % 2):44 * (w % 2) + 44, 1 + w // 2, :], taps[w]).then_inc(S["vec_in"], 16)
            sp.dma_start(vecs[44:88, 2, :], t["conv_b"][0].rearrange("(j c) -> j c", c=P)).then_inc(S["vec_in"], 16)
            past = t["state_conv"][0, 0].rearrange("w (j c) -> w j c", c=P)
            for w in range(2):
                sp.dma_start(vecs[44 * w:44 * w + 44, 3, :], past[w]).then_inc(S["vec_in"], 16)
            for n, name in enumerate(("lam_q1", "lam_q2", "lam_k1", "lam_k2")):
                sp.dma_start(lamt[:, n:n + 1], t[name][0].rearrange("(c a) -> c a", a=1)).then_inc(S["vec_in"], 16)
            def gate_column(n):
                return C_RG + n * P if n < 8 else C_GA + (n - 8) * P

            for j in range(RAW, FIRST):
                weights(0, j, w_in[:, :, gate_column(j):gate_column(j) + P])
            for h in range(HEADS):
                at = (C_RQ + h * DK, C_RK + h * DK, C_RV + h * DV, C_RV + h * DV + P, gate_column(FIRST + h))
                for j, c in enumerate(at):
                    weights(0, U_RET + 5 * h + j, w_in[:, :, c:c + P])
            with sp.Fori(0, HEADS // 2) as g:
                for h in range(2):
                    gate = gate_column(A_DIFF)
                    for j, c in enumerate((C_DQ, C_DQ + P, C_DK, C_DK + P, C_DV, C_DV + P, gate, gate + P)):
                        weights(g * 16 + U_DIFF, 8 * h + j, w_in[:, :, bass.ds(g * (4 * P) + (c + h * 2 * P), P)])
            for b, name in enumerate(("w_ret_br", "w_da_br", "w_out")):
                with sp.Fori(0, 2) as g:
                    for j in range(4):
                        weights(g * 4 + (U_B + 8 * b), j, w_of[name][:, :, bass.ds(g * (4 * P) + j * P, P)])
            with sp.Fori(0, FT // 2) as g:
                for j in range(4):
                    c = (j % 2) * FF + (j // 2) * P
                    weights(g * 4 + U_UP, j, w_of["w_up"][:, :, bass.ds(g * (2 * P) + c, P)])
            def down_weights(before, j, at):
                k = 8 * (j % 3)
                weights(before, j, w_of["w_down"][:, k:min(k + 8, FT), bass.ds(at + (j // 3) * P, P)])

            for j in range(6):
                down_weights(U_DOWN, j, 0)
            for g in range(4):
                sp.wait_ge(S["a_used"], USED_UP + -(-hid_group(g)[1] * THIRD // NT))
                sp.wait_ge(S["hid_st"], 32 * (hid_group(g)[1] + 1))
                load_hidden(sp, g, 0)
            for j in range(6, 12):
                down_weights(U_DOWN, j, 0)
            for j in range(12):
                down_weights(U_DOWN + 12, j, 4 * P)
            with sp.Fori(1, 3) as third:
                with sp.Fori(0, 2) as g:
                    for j in range(12):
                        down_weights(third * 24 + g * 12 + U_DOWN, j, g * (4 * P))
            for j in range(2):
                weights(U_PLE, j, w_of["w_ple"][:, :, j * 512:(j + 1) * 512])
            for j in range(8):
                weights(U_PG - 2, j + 2, w_of["w_ple_gate"][:, :, j * P:(j + 1) * P])

        @block.gpsimd
        def _(pool):
            def split(before, j, slot, words=8 * P, others=0):
                landed = (before + (j - j % RAW)) * 4 + 16
                pool.wait_ge(w_landed[j % RAW], landed)
                pool.sem_inc(S["w_begun"], 1)
                raw, hi, lo = w_raw[:, j % RAW, 0:words], w_hi[:, slot, 0:words], w_lo[:, slot, 0:words]
                pool.tensor_scalar(hi, raw, 1.0, 0.0, ALU.mult, ALU.add).then_inc(S["w_hi_done"], 1)
                pool.wait_ge(S["w_hi_done"], before + (j + 1 - others))
                pool.tensor_tensor(lo, raw, hi.bitcast(F32), ALU.subtract).then_inc(S["w_split"], 1)

            for j in range(8):
                split(0, j, j)
            for j in range(8, FIRST):
                pool.wait_ge(S["acc_done"], j - 7)
                split(0, j, j - 8)
            for h in range(HEADS):
                for j in range(4):
                    if h:
                        pool.wait_ge(S["ret_proj"], h * TILES)
                    else:
                        pool.wait_ge(S["acc_done"], 4 + j + 1)
                    split(0, U_RET + 5 * h + j, 4 + j)
                pool.wait_ge(S["acc_done"], FIRST + h)
                split(0, U_RET + 5 * h + 4, RET_GATE_SLOT)
            def diff_units(before, gates_done):
                for j in range(6):
                    split(before, j, j)
                pool.wait_ge(S["acc_done"], gates_done)
                for j in range(6, 8):
                    split(before, j, j)

            for j in range(6):
                if j == 3:
                    pool.wait_ge(S["acc_done"], A_DIFF)
                if j == 4:
                    pool.wait_ge(S["ret_proj"], HEADS * TILES)
                split(U_DIFF, j, j)
            for j in range(6, 8):
                split(U_DIFF, j, j)
            with pool.Fori(1, HEADS) as h:
                pool.wait_ge(S["pb_done"], h * TILES)
                diff_units(h * 8 + U_DIFF, h * 2 + A_DIFF)
            pool.wait_ge(S["pb_done"], HEADS * TILES)
            for j in range(8):
                if j == 6:
                    pool.wait_ge(S["acc_done"], GATES)
                split(U_B, j, j)
            def eight_units(g):
                for j in range(8):
                    pool.wait_ge(S["acc_done"], g * 8 + (A_B1 + j - 7))
                    split(g * 8 + U_B, j, j)

            def lo_pieces(norm, split0):
                for n in range(24):
                    if on_pool(norm, n):
                        c, k = n // KT, n % KT
                        pool.wait_ge(S["hi_done"], split0 + n + 1)
                        pool.tensor_tensor(third_of(alo(k), c), third_of(apre(k), c), third_of(ahi(k), c).bitcast(F32),
                                           ALU.subtract).then_inc(S["lo_pool"], 1)

            with pool.Fori(1, 3) as g:
                eight_units(g)
            eight_units(3)
            lo_pieces(0, L_FFN)
            with pool.Fori(4, (U_DOWN - U_B) // 8) as g:
                eight_units(g)
            for j in range(U_DOWN - 4, U_DOWN):
                pool.wait_ge(S["acc_done"], j - U_B + A_B1 - 7)
                split(0, j, j % SLOTS)
            for j in range(8):
                pool.wait_ge(S["acc_done"], A_PLE - 7 + j)
                split(U_DOWN, j, (U_DOWN + j) % SLOTS, words=down_words(j))

            def down_lo(before, j):
                slot, words = (U_DOWN + j) % SLOTS, down_words(j)
                pool.wait_ge(S["down_hi"], before + (j - 7))
                pool.tensor_tensor(w_lo[:, slot, 0:words], w_raw[:, j % RAW, 0:words],
                                   w_hi[:, slot, 0:words].bitcast(F32), ALU.subtract).then_inc(S["w_split"], 1)

            for j in range(8, 24):
                down_lo(0, j)
            with pool.Fori(1, 3) as third:
                for j in range(24):
                    down_lo(third * 24, j)
            for j in range(2):
                pool.wait_ge(S["down_done"], 22)
                split(U_PLE, j, 4 + j, others=64)
            for m in range(8):
                if m < 3:
                    pool.wait_ge(S["down_done"], 23 if m < 2 else 24)
                if m == 2:
                    lo_pieces(1, H_PLE)
                if m >= 3:
                    pool.wait_ge(S["acc_done"], A_PLE + 2 * (m - 3) + 2)
                split(U_PLE, 2 + m, PG_SLOTS[m % 3], others=64)

        @block.tensor
        def _(pe):
            def three(out, lhs, rhs, start, stop):
                pe.matmul(out, lhs[0], rhs[0], start=start, stop=False)
                pe.matmul(out, lhs[0], rhs[1], start=False, stop=False)
                return pe.matmul(out, lhs[1], rhs[0], start=False, stop=stop)

            def bank_piece(n, slot, k, c):
                at = slice(k * NT + c * THIRD, k * NT + (c + 1) * THIRD)
                return three(acc(n)[:, c, :], (wk(w_hi, slot, k), wk(w_lo, slot, k)),
                             (a_hi[:, at], a_lo[:, at]), k == 0, k == KT - 1)

            def feature_tile(n, slot, release=False):
                for k in range(KT):
                    for c in range(3):
                        last = bank_piece(n, slot, k, c)
                    if release and k < KT - 1:
                        last.then_inc(S["a_used"], 1)
                return last

            def wait_split(norm, ready, n):
                if on_pool(norm, n):
                    pe.wait_ge(S["lo_pool"], norm * pieces_before(0, 24, True) + pieces_before(norm, n, True) + 1)
                else:
                    pe.wait_ge(S["lo_done"], ready + pieces_before(norm, n, False) + 1)

            def first_pair(n, slot, ready, by_thirds):
                if by_thirds:
                    for c in range(3):
                        for m in range(2):
                            for k in range(KT):
                                if m == 0:
                                    wait_split(0, ready, c * KT + k)
                                last = bank_piece(n + m, slot + m, k, c)
                            if c == 2:
                                last.then_inc(S["acc_done"], 1)
                else:
                    for k in range(KT):
                        pe.wait_ge(S["lo_done"], ready + k + 1)
                        for m in range(2):
                            for c in range(3):
                                last = bank_piece(n + m, slot + m, k, c)
                            if k == KT - 1:
                                last.then_inc(S["acc_done"], 1)

            pe.wait_ge(S["const_in"], 16)
            pe.wait_ge(S["gain_in"], 16 * 4)
            pe.transpose(ps[:, 7, 0:26], vecs[0:26, 0, :], ident[0:26, 0:26]).then_inc(S["gain_tr"], 1)

            def transposes(src, bank, r):
                for k in range(KT):
                    last = pe.transpose(ps[:, bank + k // 4, (k % 4) * P:(k % 4) * P + r],
                                        src[0:r, k * P:(k + 1) * P], ident[0:r, 0:r])
                return last

            def first_gate_third(c, tiles):
                pe.wait_ge(S["w_split"], 1)
                pe.wait_ge(S["lo_done"], tiles)
                for k in range(KT):
                    last = bank_piece(0, 0, k, c)
                return last

            for step in range(TILES + 1):
                i = step
                if i < TILES:
                    pe.wait_ge(x_landed[i % 3], 16 * (i // 3 + 1))
                    if i >= 1:
                        pe.wait_ge(S["x_ev_a"], i)
                        pe.wait_ge(S["x_ev_d"], i)
                    transposes(xin[:, i % 3, :], 3, rows(i)).then_inc(S["x_tr"], 1)
                i = step - 1
                if i >= 0:
                    pe.wait_ge(S["xn_done"], i + 1)
                    if i >= 1:
                        pe.wait_ge(S["pre_done"], i)
                    transposes(xn[:, i % 2, :], 5, rows(i)).then_inc(S["xn_tr"], 1)
                if step == 6:
                    first_gate_third(0, 3)
                if step == 9:
                    first_gate_third(1, 6)
            first_gate_third(2, TILES).then_inc(S["acc_done"], 1)
            pe.wait_ge(S["vec_in"], 16 * 10)
            pe.wait_ge(S["gain_ev"], 1)
            for b in range(1, 4):
                last = pe.transpose(ps[:, 7, b * P:b * P + 88], vecs[0:88, b, :], ident[0:88, 0:88])
            last.then_inc(S["vec_tr"], 1)
            pe.wait_ge(S["lam_m"], 2)
            pe.wait_ge(S["pre_done"], TILES)
            pe.matmul(ps[:, 6, 0:2], ones[:, :], lamt[:, 4:6], start=True, stop=True).then_inc(S["lam_s"], 1)

            def sum_over_features(n, c, ready):
                pe.wait_ge(S["ssq_done"], ready)
                pe.matmul(acc(n)[:, c, :], ones[:, :], third_of(row(0), c),
                          start=True, stop=True).then_inc(S["ssq_bc"], 1)

            pe.wait_ge(S["x_ev_a"], TILES)
            pe.wait_ge(S["x_ev_d"], TILES)
            for j in range(1, FIRST):
                pe.wait_ge(S["w_split"], j + 1)
                if j >= 2:
                    pe.wait_ge(S["acc_free"], j - 1)
                feature_tile(j, j % SLOTS).then_inc(S["acc_done"], 1)
            pe.wait_ge(S["acc_free"], FIRST)

            def gate_third(bank, slot, c):
                for k in range(KT):
                    at = slice(k * NT + c * THIRD, k * NT + (c + 1) * THIRD)
                    last = three(ps[:, bank, 0:THIRD], (wk(w_hi, slot, k), wk(w_lo, slot, k)),
                                 (a_hi[:, at], a_lo[:, at]), k == 0, k == KT - 1)
                return last

            def project(bank, i, s0, s1, k0=0, k1=KT):
                r, n = rows(i), (s1 - s0) * P
                out = ps[0:r, bank, 0:n].rearrange("p (s c) -> p s c", c=P)
                for k in range(k0, k1):
                    cut = slice(k * NT + i * P, k * NT + i * P + r)
                    last = three(out, (a_hi[:, cut], a_lo[:, cut]),
                                 (w_hi[:, s0:s1, k * P:(k + 1) * P], w_lo[:, s0:s1, k * P:(k + 1) * P]),
                                 k == 0, k == KT - 1)
                return last

            def begun(i):
                if i == LAST:
                    pe.sem_inc(S["tail_begun"], 1)

            with pe.Fori(0, HEADS) as h:
                c9 = h * TILES
                for step in range(TILES + 4):
                    i = step
                    if i < TILES:
                        if i == 0:
                            pe.wait_ge(S["w_split"], h * 5 + (U_RET + 4))
                        if i >= 3:
                            pe.wait_ge(S["rope_done"], h * (2 * TILES) + 2 * (i - 2))
                        project(i % 3, i, 4, 8).then_inc(S["ret_proj"], 1)
                    c = step - TILES
                    if 0 <= c < 3:
                        if c == 0:
                            pe.wait_ge(S["w_split"], h * 5 + (U_RET + 5))
                        pe.wait_ge(S["v_done"], c9 + (7 + c))
                        pe.wait_ge(S["rope_done"], h * (2 * TILES) + 2 * (7 + c))
                        gate_third(c, RET_GATE_SLOT, c).then_inc(S["acc_done" if c == 2 else "gate_part"], 1)
                    i = step - 1
                    if 0 <= i < TILES:
                        r = rows(i)
                        pe.wait_ge(S["rope_done"], h * (2 * TILES) + 2 * (i + 1))
                        if i >= 1:
                            pe.wait_ge(S["qk_ev"], c9 + i)
                        begun(i)
                        for m in range(2):
                            last = pe.transpose(ps[:, 4, m * P:m * P + r], qk[0:r, i % 2, m * P:(m + 1) * P],
                                                ident[0:r, 0:r])
                        last.then_inc(S["qk_tr"], 1)
                    i = step - 2
                    if 0 <= i < TILES:
                        r = rows(i)
                        pe.wait_ge(S["qk_ev"], c9 + (i + 1))
                        if i >= 1:
                            pe.wait_ge(S["sm_done"], c9 + i)
                        begun(i)
                        pe.matmul(ps[0:r, 5, 0:r], qk_t[:, i % 2, P:P + r], qk_t[:, i % 2, 0:r],
                                  start=True, stop=True).then_inc(S["sc_done"], 1)
                    i = step - 3
                    if 0 <= i < TILES:
                        r = rows(i)
                        pe.wait_ge(S["sm_done"], c9 + (i + 1))
                        pe.wait_ge(S["v_done"], c9 + (i + 1))
                        pe.wait_ge(S["kd_done"], c9 + (i + 1))
                        pe.wait_ge(S["qd_done"], c9 + (i + 1))
                        if i >= 1:
                            pe.wait_ge(S["o_nrm"], c9 + i)
                            pe.wait_ge(S["state_done"], c9 + i)
                        else:
                            pe.wait_ge(S["head_in"], h * 64 + 64)
                        begun(i)
                        out = ps[0:r, 6, 0:DV]
                        last = pe.matmul(out, s_m[0:r, i % 2, 0:r], v_tok[0:r, i, :], start=True, stop=i == 0)
                        if i:
                            last = pe.matmul(out, q_d[:, i % 2, 0:r], s_p if i < LAST else s_s, start=False, stop=True)
                        last.then_inc(S["o_done"], 1)
                        pe.matmul(ps[:, 7, 0:DV], kd[0:r, i % 3, :], v_tok[0:r, i, :],
                                  start=True, stop=True).then_inc(S["kv_done"], 1)
                    i = step - 4
                    if 0 <= i < TILES:
                        r = rows(i)
                        pe.wait_ge(S["o_nrm"], c9 + (i + 1))
                        if i >= 1:
                            pe.wait_ge(S["ot_ev"], c9 + i)
                        begun(i)
                        for m in range(2):
                            last = pe.transpose(ps[:, 3, m * P:m * P + r],
                                                o_n[0:r, i % 2, m * P:(m + 1) * P], ident[0:r, 0:r])
                        last.then_inc(S["ot_tr"], 1)
                pe.wait_ge(S["ot_ev"], c9 + TILES)
                pe.wait_ge(S["state_done"], c9 + TILES)
                pe.wait_ge(S["acc_free"], h + (FIRST + 1))

            with pe.Fori(0, HEADS) as h:
                c9 = h * TILES

                def gate_fill(n):
                    if n % 3 == 0:
                        pe.wait_ge(S["w_split"], h * 8 + (U_DIFF + 7 + n // 3))
                    if n < 3:
                        pe.wait_ge(S["d_nrm"], h * (4 * TILES) + 4 * (TILES - (n == 0)))
                        pe.wait_ge(S["d_v"], c9 + (TILES - (n == 0)))
                    elif n == 3:
                        pe.wait_ge(S["dc_ev"], h + 1)
                    else:
                        wait_piece(pe, h, n - 4, S["acc_free"], S["gate_ev"])
                    last = gate_third((3 + n) % 4, DIFF_GATE_SLOT + n // 3, n % 3)
                    last.then_inc(S["acc_done" if n % 3 == 2 else "gate_part"], 1)

                for step in range(DIFF_STEPS):
                    def scores(m, i):
                        keys, first = (P * (i + 1), 0) if i < LAST else (NS + PAST, NP)
                        r = rows(i)
                        for b in range(0, keys, 512):
                            n = min(512, keys - b)
                            diag = i < LAST and b + n == keys
                            last = pe.matmul(ps[0:r, 5 + b // 512, 0:n], q_t[:, i % 2, m, 0:r],
                                             k_t[:, m, first + b:first + b + n], start=True, stop=not diag)
                            if diag:
                                last = pe.matmul(ps[0:r, 5 + b // 512, n - P:n], mask[0:1, 0:P], mask[0:1, P:2 * P],
                                                 start=False, stop=True)
                        return last

                    def blocks(i):
                        if i < LAST:
                            return [(P, b * P, b) for b in range(i + 1)]
                        return [(NS, 0, LAST), (P, NS, TILES)]

                    def transpose_a(i, b0, b1):
                        r = rows(i)
                        for b in range(b0, b1):
                            n, c, _ = blocks(i)[b]
                            last = pe.transpose(ps[0:n, 4, (b % 4) * P:(b % 4) * P + r], a_w[0:r, c:c + n],
                                                ident[0:r, 0:r])
                        return last

                    def weigh_v(i, b0, b1):
                        r, every = rows(i), len(blocks(i))
                        for b in range(b0, b1):
                            n, _, vt = blocks(i)[b]
                            last = pe.matmul(ps[0:r, 7, 0:DV], a_t[0:n, b, 0:r], v_tok[0:n, vt, :],
                                             start=b == 0, stop=b == every - 1)
                        return last

                    i = step
                    if i < TILES:
                        if i == 0:
                            pe.wait_ge(S["w_split"], h * 8 + (U_DIFF + 3))
                        if i >= 2:
                            pe.wait_ge(S["d_nrm"], h * (4 * TILES) + 4 * (i - 1))
                            pe.wait_ge(S["d_v"], c9 + (i - 1))
                        project(2 * (i % 2), i, 0, 3, k1=EARLY)
                    i = step - 2
                    if 0 <= i < TILES:
                        pe.wait_ge(S["d_ev"], h * (2 * TILES) + 2 * (i + 1))
                        if i == LAST:
                            pe.wait_ge(S["dc_ev"], h + 1)
                        if i >= 1:
                            pe.wait_ge(S["e1_done"], c9 + i)
                        begun(i)
                        scores(0, i).then_inc(S["s0_done"], 1)
                    i = step - 3
                    if 0 <= i < TILES:
                        every = len(blocks(i))
                        pe.wait_ge(S["a_done"], c9 + (i + 1))
                        if i + 1 < TILES:
                            pe.wait_ge(S["d_ev"], h * (2 * TILES) + 2 * (i + 2))
                        begun(i)
                        transpose_a(i, 0, min(4, every)).then_inc(S["at0_tr"], 1)
                    i = step
                    if i < TILES:
                        project(2 * (i % 2), i, 0, 3, k0=EARLY).then_inc(S["pa_done"], 1)
                    if i == TILES:
                        pe.wait_ge(S["d_in"], h * 32 + 32)
                        pe.wait_ge(S["d_nrm"], h * (4 * TILES) + 4 * (TILES - 1))
                        for m in range(2):
                            last = pe.transpose(ps[:, 2, m * P:(m + 1) * P], kc[:, m * P:(m + 1) * P], ident[:, :])
                        last.then_inc(S["dc_tr"], 1)
                    if TILES <= i < TILES + 3:
                        gate_fill(2 * (i - TILES))
                    i = step - 3
                    if 0 <= i < TILES:
                        pe.wait_ge(S["at0_ev"], c9 + (i + 1))
                        if i >= 1:
                            pe.wait_ge(S["do_nrm"], c9 + i)
                        if i >= 2:
                            pe.wait_ge(S["dot_ev"], h * (2 * TILES) + 2 * (i - 1))
                        begun(i)
                        last = weigh_v(i, 0, min(4, every))
                        if every <= 4:
                            last.then_inc(S["pv_done"], 1)
                        else:
                            transpose_a(i, 4, every).then_inc(S["at1_tr"], 1)
                    i = step - 2
                    if 0 <= i < TILES:
                        pe.wait_ge(S["e0_done"], c9 + (i + 1))
                        begun(i)
                        scores(1, i).then_inc(S["s1_done"], 1)
                    i = step
                    if i < TILES:
                        if i == 0:
                            pe.wait_ge(S["w_split"], h * 8 + (U_DIFF + 6))
                        project(2 * (i % 2) + 1, i, 3, 6).then_inc(S["pb_done"], 1)
                    if TILES <= i < TILES + 3:
                        gate_fill(2 * (i - TILES) + 1)
                    i = step - 1
                    if 0 <= i < TILES:
                        r = rows(i)
                        pe.wait_ge(S["d_rope"], h * (2 * TILES) + 2 * (i + 1))
                        if 4 <= step - 3 < LAST:
                            pe.wait_ge(S["at1_ev"], h * 4 + (step - 3 - 3))
                        begun(i)
                        for m in range(4):
                            last = pe.transpose(ps[:, 4, m * P:m * P + r], qk[0:r, i % 2, m * P:(m + 1) * P],
                                                ident[0:r, 0:r])
                        last.then_inc(S["d_tr"], 1)
                    i = step - 3
                    if 0 <= i < TILES and every > 4:
                        pe.wait_ge(S["at1_ev"], h * 4 + (i - 3))
                        weigh_v(i, 4, every).then_inc(S["pv_done"], 1)
                    i = step - 4
                    if 0 <= i < TILES:
                        r = rows(i)
                        pe.wait_ge(S["do_nrm"], c9 + (i + 1))
                        if i >= 1:
                            pe.wait_ge(S["dot_ev"], h * (2 * TILES) + 2 * i)
                        begun(i)
                        for m in range(2):
                            last = pe.transpose(ps[:, 7, (2 + m) * P:(2 + m) * P + r],
                                                o_n[0:r, i % 2, m * P:(m + 1) * P], ident[0:r, 0:r])
                        last.then_inc(S["dot_tr"], 1)
                pe.wait_ge(S["dot_ev"], h * (2 * TILES) + 2 * TILES)
                pe.wait_ge(S["acc_free"], h * 2 + (A_DIFF + 2))
                pe.wait_ge(S["gate_ev"], h * 4 + (2 * HEADS + 4))

            for b in range(3):
                n, u = A_B1 + 8 * b, U_B + 8 * b
                pe.wait_ge(S["w_split"], u + 2)
                pe.wait_ge(S["acc_free"], n)
                first_pair(0, 0, L_B1 + 8 * b, False)
                for j in range(2, 8):
                    pe.wait_ge(S["w_split"], u + j + 1)
                    pe.wait_ge(S["acc_free"], n + j - 1)
                    feature_tile(j, j, release=j == 7 and b < 2).then_inc(S["acc_done"], 1)
            pe.wait_ge(S["acc_free"], A_UP - 1)
            for c in range(3):
                sum_over_features(0, c, 6 + c + 1)
            pe.wait_ge(S["w_split"], U_UP + 2)
            pe.wait_ge(S["rms_rt"], 3)
            pe.wait_ge(S["acc_free"], A_UP)
            first_pair(0, 0, L_FFN, True)
            for j in range(2, 8):
                pe.wait_ge(S["w_split"], U_UP + j + 1)
                pe.wait_ge(S["acc_free"], A_UP + j - 1)
                feature_tile(j, j).then_inc(S["acc_done"], 1)
            with pe.Fori(1, 2 * FT // 8) as g:
                for j in range(8):
                    pe.wait_ge(S["w_split"], g * 8 + (U_UP + j + 1))
                    pe.wait_ge(S["acc_free"], g * 8 + (A_UP + j - 1))
                    feature_tile(j, j).then_inc(S["acc_done"], 1)
            for j in range(2 * FT - 4, 2 * FT):
                pe.wait_ge(S["w_split"], U_UP + j + 1)
                pe.wait_ge(S["acc_free"], A_UP + j - 1)
                feature_tile(j, j % SLOTS, release=j == 2 * FT - 1).then_inc(S["acc_done"], 1)
            def down_piece(m, k):
                slot = (U_DOWN + 3 * m + k // 8) % SLOTS
                at = slice(k * THIRD, (k + 1) * THIRD)
                return three(ps[:, (m + 6) % 8, 0:THIRD], (wk(w_hi, slot, k % 8), wk(w_lo, slot, k % 8)),
                             (a_hi[:, at], a_lo[:, at]), k == 0, k == FT - 1)

            with pe.Fori(0, 3) as third:
                pe.wait_ge(S["down_free"], third * 8 + 2)
                for k in range(FT):
                    if k % 8 == 0:
                        pe.wait_ge(S["w_split"], third * 24 + (U_DOWN + 3 + k // 8 + 1))
                    pe.wait_ge(S["lo_done"], third * FT + (L_DOWN + k + 1))
                    for m in range(2):
                        last = down_piece(m, k)
                        if k == FT - 1:
                            last.then_inc(S["down_done"], 1)
                pe.wait_ge(S["acc_free"], A_PLE)
                for m in range(2, 8):
                    pe.wait_ge(S["down_free"], third * 8 + (m + 1))
                    for k in range(FT):
                        if k % 8 == 0:
                            pe.wait_ge(S["w_split"], third * 24 + (U_DOWN + 3 * m + k // 8 + 1))
                        last = down_piece(m, k)
                        if m == 7 and k < FT - 1:
                            last.then_inc(S["hid_used"], 1)
                    last.then_inc(S["down_done"], 1)
            def out_rows(m):
                pe.wait_ge(S["y_done"], m + 1)
                for part, (i0, i1) in enumerate(((0, 4), (4, 8), (8, 9))):
                    need = 3 * m + (0, 0, 1)[part]
                    if need:
                        pe.wait_ge(S["y_ev"], need)
                    for i in range(i0, i1):
                        r = rows(i)
                        last = pe.transpose(ps[0:r, 6 + part % 2, (i % 4) * P:(i % 4 + 1) * P],
                                            x(m)[:, i * P:i * P + r], ident[:, :])
                    last.then_inc(S["y_tr"], 1)

            def ple_transposes(b):
                for i in range(2 * b, min(2 * b + 2, TILES)):
                    r = rows(i)
                    for k in range(2):
                        at = (2 * k + i % 2) * P
                        last = pe.transpose(ps[:, 6 + b % 2, at:at + r], ple_in[0:r, i, k * P:(k + 1) * P],
                                            ident[0:r, 0:r])
                last.then_inc(S["ple_tr"], 1)

            pe.wait_ge(S["ple_in"], 32)
            ple_transposes(0)
            ple_transposes(1)
            pe.wait_ge(S["u_last_done"], 2 * FT)
            pe.wait_ge(S["down_free"], 8 * 3 + 6)
            for b in range(2):
                flat = u_last[:, b * FT:(b + 1) * FT, :].rearrange("p j w -> p (j w)")
                last = pe.transpose(ps[0:4 * FT, 0, b * P:(b + 1) * P], flat, ident[:, :])
            last.then_inc(S["ul_tr"], 1)
            pe.wait_ge(S["down_free"], 8 * 3 + 7)
            sum_over_features(1, 0, SSQ_DOWN + 7)
            pe.wait_ge(S["down_free"], 8 * 4)
            sum_over_features(1, 1, SSQ_DOWN + 14)
            for b in range(2, 5):
                pe.wait_ge(S["ple_lo"], b - 1)
                ple_transposes(b)
            sum_over_features(1, 2, SSQ_DOWN + 21)
            pe.wait_ge(S["ple_lo"], 5)
            def gate_product(m):
                pe.wait_ge(S["w_split"], U_PG + m + 1)
                if m:
                    pe.wait_ge(S["sig_done"], m)
                    feature_tile(1, PG_SLOTS[m % 3]).then_inc(S["acc_done"], 1)
                else:
                    pe.wait_ge(S["rms_rt"], 6)
                    for c in range(3):
                        for k in range(KT):
                            wait_split(1, L_PLE, c * KT + k)
                            last = bank_piece(1, PG_SLOTS[0], k, c)
                    last.then_inc(S["acc_done"], 1)

            def ple_product(m):
                if m == 0:
                    pe.wait_ge(S["w_split"], U_PLE + 2)
                    pe.wait_ge(S["ul_ev"], 1)
                else:
                    pe.wait_ge(S["y_mul"], m)
                for k in range(2):
                    at = k * 512 + (m % 4) * P
                    for c in range(3):
                        cut = slice(k * NT + c * THIRD, k * NT + (c + 1) * THIRD)
                        last = three(acc(0)[:, c, :],
                                     (w_hi[:, 4 + m // 4, at:at + P], w_lo[:, 4 + m // 4, at:at + P]),
                                     (ple_hi[:, cut], ple_lo[:, cut]), k == 0, k == 1)
                last.then_inc(S["acc_done"], 1)

            ple_product(0)
            gate_product(0)
            for m in range(1, 8):
                gate_product(m)
                ple_product(m)
                out_rows(m - 1)
            out_rows(7)

        @block.scalar
        def _(act):
            full_k = full[:, :].rearrange("p (k n) -> p k n", k=KT)
            for step in range(TILES + 2):
                i = step
                if i < TILES:
                    r, b = rows(i), i % 2
                    act.wait_ge(x_landed[i % 3], 16 * (i // 3 + 1))
                    if i >= 2:
                        act.wait_ge(S["xn_tr"], i - 1)
                    act.activation(xn[0:r, b, :], xin[0:r, i % 3, :], ACT.Square,
                                   accum_out=st[0:r, b:b + 1]).then_inc(S["xs_done"], 1)
                    act.wait_ge(S["xs_done"], i + 1)
                    if i == 0:
                        act.wait_ge(S["lam_m"], 1)
                    if i >= 2:
                        act.wait_ge(S["xi_done"], i - 1)
                    act.activation(st[0:r, 2 + b:3 + b], st[0:r, b:b + 1], ACT.Sqrt, bias=eps[0:r, 0:1],
                                   scale=1.0 / D).then_inc(S["xr_done"], 1)
                    act.wait_ge(S["x_tr"], i + 1)
                    act.copy(full_k[:, 0:4, i * P:i * P + r],
                             ps[:, 3, :].rearrange("p (k c) -> p k c", k=4)[:, :, 0:r]).then_inc(S["x_ev_a"], 1)
                i = step - 2
                if i >= 0:
                    r = rows(i)
                    act.wait_ge(S["pre_done"], i + 1)
                    act.activation(a_hi_k[:, :, i * P:i * P + r], a_pre_k[:, :, i * P:i * P + r],
                                   ACT.Copy).then_inc(S["hi_done"], 1)
            act.wait_ge(S["x_ev_a"], TILES)
            act.wait_ge(S["x_ev_d"], TILES)
            act.dma_start(xt_d.rearrange("k p n -> p k n"), full_k).then_inc(S["xt_st"], 16)
            act.wait_ge(S["lam_s"], 1)
            act.activation(lamt[:, 6:8], ps[:, 6, 0:2], ACT.Exp).then_inc(S["lam_e"], 1)

            def roots_of_means(n, before):
                for c in range(3):
                    act.wait_ge(S["ssq_bc"], before + c + 1)
                    act.activation(third_of(row(0), c), acc(n)[:, c, :], ACT.Sqrt, bias=eps[:, 0:1],
                                   scale=1.0 / D).then_inc(S["rms_rt"], 1)

            def hi_of_scaled(pre0):
                for c in range(3):
                    for k in range(KT):
                        act.wait_ge(S["pre_done"], pre0 + c * KT + k + 1)
                        act.activation(third_of(ahi(k), c), third_of(apre(k), c),
                                       ACT.Copy).then_inc(S["hi_done"], 1)

            def gate(before, j, func, ring=True):
                act.wait_ge(S["acc_done"], before + (j + 1))
                if ring:
                    act.wait_ge(gate_st[j], before * 8)
                act.activation(thirds(row(3 + j)), acc(j), func).then_inc(S["acc_free"], 1)
                act.wait_ge(S["acc_free"], before + (j + 1))
                act.dma_start(gates_d[bass.ds(before + j, 1)].rearrange("k p n -> p (k n)"), row(3 + j)).then_inc(gate_st[j], 16)

            for j in range(2):
                gate(0, j, ACT.Silu, ring=False)
            with act.Fori(1, 4) as g:
                for j in range(2):
                    gate(g * 2, j, ACT.Silu)
            with act.Fori(4, FIRST // 2) as g:
                for j in range(2):
                    gate(g * 2, j, ACT.Copy)
            act.wait_ge(gate_st[0], FIRST // 2 * 16)
            act.wait_ge(gate_st[1], FIRST // 2 * 16)

            act.wait_ge(S["xt_st"], 16)
            act.wait_ge(S["lo_done"], TILES)
            act.dma_start(cos, t["c_cos"]).then_inc(S["head_const"], 16)
            act.dma_start(sin, t["c_sin"]).then_inc(S["head_const"], 16)
            act.dma_start(gqk[:, 0, :], t["g_qn"][0].partition_broadcast(P)).then_inc(S["head_const"], 16)
            act.dma_start(gqk[:, 1, :], t["g_kn"][0].partition_broadcast(P)).then_inc(S["head_const"], 16)
            act.dma_start(mask[0:1, :], t["c_mask"]).then_inc(S["head_const"], 16)

            with act.Fori(0, HEADS) as h:
                c9 = h * TILES
                act.dma_start(hc, t["c_ret"][bass.ds(h, 1)].rearrange("h p c -> p (h c)")).then_inc(S["head_in"], 16)
                act.dma_start(s_s, t["state_ret"][0, 0][bass.ds(h, 1)].rearrange("h p c -> p (h c)")).then_inc(S["head_in"], 16)
                for m in range(2):
                    act.dma_start(gates_h[m], gates_d[bass.ds(h * 2 + m, 1)].rearrange("k p n -> p (k n)")).then_inc(S["head_in"], 16)
                for step in range(TILES + 4):
                    i = step
                    if i < TILES:
                        r = rows(i)
                        act.wait_ge(S["ret_proj"], c9 + (i + 1))
                        act.copy(v_tok[0:r, i, :], ps[0:r, i % 3, 2 * P:4 * P]).then_inc(S["v_done"], 1)
                    i = step - 1
                    if 0 <= i < TILES:
                        r = rows(i)
                        act.wait_ge(S["qk_tr"], c9 + (i + 1))
                        if i >= 2:
                            act.wait_ge(S["sc_done"], c9 + (i - 1))
                            act.wait_ge(S["qd_done"], c9 + (i - 1))
                        act.copy(qk_t[:, i % 2, :].rearrange("p (m n) -> p m n", m=2)[:, :, 0:r],
                                 ps[:, 4, 0:2 * P].rearrange("p (m n) -> p m n", m=2)[:, :, 0:r]).then_inc(S["qk_ev"], 1)
                    i = step - 3
                    if 0 <= i < TILES:
                        r, b = rows(i), i % 2
                        act.wait_ge(S["o_done"], c9 + (i + 1))
                        if i >= 2:
                            act.wait_ge(S["ot_tr"], c9 + (i - 1))
                        act.activation(o_n[0:r, b, :], ps[0:r, 6, 0:DV], ACT.Square,
                                       accum_out=st[0:r, b:b + 1]).then_inc(S["o_sq"], 1)
                        act.wait_ge(S["o_sq"], c9 + (i + 1))
                        act.activation(st[0:r, 2 + b:3 + b], st[0:r, b:b + 1], ACT.Sqrt, bias=eps[0:r, 0:1],
                                       scale=1.0 / DV).then_inc(S["o_rt"], 1)
                        act.wait_ge(S["o_inv"], c9 + (i + 1))
                        act.activation(o_n[0:r, b, :], ps[0:r, 6, 0:DV], ACT.Copy,
                                       scale=st[0:r, 4 + b:5 + b]).then_inc(S["o_nrm"], 1)
                    i = step - 4
                    if 0 <= i < TILES:
                        r, b = rows(i), i % 2
                        act.wait_ge(S["ot_ev"], c9 + (i + 1))
                        act.dma_start(o_d[bass.ds(h * 2, 2), :, i * P:i * P + r].rearrange("m p n -> p m n"),
                                      o_t[:, b, :, 0:r]).then_inc(ot_st[b], 16)
                for i, s_x, name in ((LAST - 1, s_p, "ret_prompt"), (LAST, s_s, "ret_sample")):
                    act.wait_ge(S["state_done"], c9 + (i + 1))
                    act.dma_start(t[name][0, 0][bass.ds(h, 1)].rearrange("h p c -> p (h c)"), s_x).then_inc(S["s_out"], 16)
                act.wait_ge(S["acc_free"], h + (FIRST + 1))
                act.dma_start(gates_d[bass.ds(h + FIRST, 1)].rearrange("k p n -> p (k n)"), gate_row).then_inc(gate_st[0], 16)
                act.wait_ge(gate_st[0], h * 16 + (FIRST // 2 * 16 + 16))
                act.wait_ge(S["s_out"], h * 32 + 32)
                act.wait_ge(ot_st[0], h * (16 * 5) + 16 * 5)
                act.wait_ge(ot_st[1], h * (16 * 4) + 16 * 4)

            def load_side(q, src):
                act.dma_start(side(q), src).then_inc(side_in[q % 3], 16)

            def branch_a_hi(k):
                act.wait_ge(side_in[(Q_A + k) % 3], 16 * ((Q_A + k) // 3 + 1))
                act.activation(ahi(k), side(Q_A + k), ACT.Copy).then_inc(S["hi_done"], 1)

            def diff_head(h, final):
                c9 = h * TILES
                act.dma_start(kc, t["cache_k"][0, 0][:, bass.ds(h, 1)].rearrange("t h m d -> t (h m d)")).then_inc(S["d_in"], 16)
                act.dma_start(v_tok[:, TILES, :], t["cache_v"][0, 0][:, bass.ds(h, 1)].rearrange("t h d -> t (h d)")).then_inc(S["d_in"], 16)
                for step in range(DIFF_STEPS):
                    if final and step == TILES + 2:
                        act.wait_ge(S["s1_done"], HEADS * TILES)
                        for q in range(2):
                            load_side(q, o_d[q])
                    i = step - 4
                    if 0 <= i < TILES:
                        r, b = rows(i), i % 2
                        act.wait_ge(S["pv_done"], c9 + (i + 1))
                        if i >= 1:
                            act.wait_ge(S["dot_tr"], c9 + i)
                        act.activation(o_n[0:r, b, :], ps[0:r, 7, 0:DV], ACT.Square,
                                       accum_out=st[0:r, b:b + 1]).then_inc(S["do_sq"], 1)
                    i = step - 1
                    if 0 <= i < TILES:
                        r, b = rows(i), i % 2
                        act.wait_ge(S["pa_done"], c9 + (i + 1))
                        if i >= 1:
                            act.wait_ge(S["d_rope"], h * (2 * TILES) + 2 * i)
                        for m in range(4):
                            if m == 3:
                                act.wait_ge(S["pb_done"], c9 + (i + 1))
                            bank, at = (2 * b, m * P) if m < 3 else (2 * b + 1, 0)
                            act.activation(nrm[0:r, m * P:(m + 1) * P], ps[0:r, bank, at:at + P], ACT.Square,
                                           accum_out=st[0:r, 8 + 4 * b + m:9 + 4 * b + m]).then_inc(S["d_sq"], 1)
                    i = step - 4
                    if 0 <= i < TILES:
                        r, b = rows(i), i % 2
                        act.wait_ge(S["do_sq"], c9 + (i + 1))
                        act.activation(st[0:r, 2 + b:3 + b], st[0:r, b:b + 1], ACT.Sqrt, bias=eps[0:r, 0:1],
                                       scale=1.0 / DV).then_inc(S["do_rt"], 1)
                    i = step - 1
                    if 0 <= i < TILES:
                        r, b = rows(i), i % 2
                        act.wait_ge(S["d_sq"], h * (4 * TILES) + 4 * (i + 1))
                        act.activation(st[0:r, 16 + 4 * b:20 + 4 * b], st[0:r, 8 + 4 * b:12 + 4 * b], ACT.Sqrt,
                                       bias=eps[0:r, 0:1], scale=1.0 / DK).then_inc(S["d_rt"], 1)
                        act.copy(v_tok[0:r, i, :], ps[0:r, 2 * b + 1, P:3 * P]).then_inc(S["d_v"], 1)
                        act.wait_ge(S["d_v"], c9 + (i + 1))
                        out = t["new_v_prompt"][0, 0, i * P:(i + 1) * P] if i < LAST else t["new_v_sample"][0, 0]
                        act.dma_start(out[:, bass.ds(h, 1)].rearrange("t h d -> t (h d)"), v_tok[0:r, i, :]).then_inc(S["v_st"], 16)
                    i = step - 4
                    if 0 <= i < TILES:
                        r, b = rows(i), i % 2
                        act.wait_ge(S["do_inv"], c9 + (i + 1))
                        act.activation(o_n[0:r, b, :], ps[0:r, 7, 0:DV], ACT.Copy,
                                       scale=st[0:r, 4 + b:5 + b]).then_inc(S["do_nrm"], 1)
                    i = step - 5
                    if 0 <= i < TILES:
                        r, b = rows(i), i % 2
                        act.wait_ge(S["dot_tr"], c9 + (i + 1))
                        if i >= 2:
                            act.wait_ge(dot_st[b], h * (16 * (5 - b)) + 16 * (i // 2))
                        for m in range(2):
                            act.activation(o_t[:, b, m, 0:r], ps[:, 7, (2 + m) * P:(2 + m) * P + r], ACT.Copy,
                                           scale=cols[:, 24 + m:25 + m]).then_inc(S["dot_ev"], 1)
                        act.wait_ge(S["dot_ev"], h * (2 * TILES) + 2 * (i + 1))
                        act.dma_start(o_d[bass.ds(h * 2 + 8, 2), :, i * P:i * P + r].rearrange("m p n -> p m n"),
                                      o_t[:, b, :, 0:r]).then_inc(dot_st[b], 16)
                    i = step - 2
                    if 0 <= i < TILES:
                        r, b = rows(i), i % 2
                        keys = P * (i + 1) if i < LAST else NS + PAST
                        act.wait_ge(S["m0_done"], c9 + (i + 1))
                        if i >= 1:
                            act.wait_ge(S["a_done"], c9 + i)
                        act.activation(e0[0:r, 0:keys], s_bank[0:r, 0:keys], ACT.Exp, bias=st[0:r, 24 + b:25 + b],
                                       accum_out=st[0:r, 28 + 2 * b:29 + 2 * b]).then_inc(S["e0_done"], 1)
                    i = step - 1
                    if 0 <= i < TILES:
                        r, b = rows(i), i % 2
                        act.wait_ge(S["d_rope"], h * (2 * TILES) + 2 * (i + 1))
                        out = t["new_k_prompt"][0, 0, i * P:(i + 1) * P] if i < LAST else t["new_k_sample"][0, 0]
                        act.dma_start(out[:, bass.ds(h, 1)].rearrange("t h m d -> t (h m d)"), qk[0:r, b, 2 * P:4 * P]).then_inc(k_st[b], 16)
                    i = step - 2
                    if 0 <= i < TILES:
                        r, b = rows(i), i % 2
                        act.wait_ge(S["m1_done"], c9 + (i + 1))
                        act.activation(e1[0:r, 0:keys], s_bank[0:r, 0:keys], ACT.Exp, bias=st[0:r, 26 + b:27 + b],
                                       accum_out=st[0:r, 29 + 2 * b:30 + 2 * b]).then_inc(S["e1_done"], 1)
                    for n in (2 * (step - TILES - 1), 2 * (step - TILES - 1) + 1):
                        if 0 <= n < 6:
                            wait_piece(act, h, n, S["acc_free"], S["gate_ev"])
                            out = gates_d[bass.ds(h * 2 + (A_DIFF + n // 3), 1), :, n % 3 * THIRD:(n % 3 + 1) * THIRD]
                            act.dma_start(out.rearrange("k p n -> p (k n)"), gate_piece(n)).then_inc(part_st[n % 2], 16)
                    if final and step == TILES + 3:
                        act.wait_ge(S["v_st"], HEADS * (16 * TILES))
                        for q in range(2, 4):
                            load_side(q, o_d[q])
                if final:
                    load_side(4, o_d[4])
                    act.wait_ge(S["acc_done"], GATES)
                    for k in range(4):
                        branch_a_hi(k)
                    load_side(6, o_d[6])
                act.wait_ge(part_st[0], h * 48 + 48)
                act.wait_ge(part_st[1], h * 48 + 48)
                act.wait_ge(S["v_st"], h * (16 * TILES) + 16 * TILES)
                for sems in (k_st, dot_st):
                    act.wait_ge(sems[0], h * (16 * 5) + 16 * 5)
                    act.wait_ge(sems[1], h * (16 * 4) + 16 * 4)

            with act.Fori(0, HEADS - 1) as h:
                diff_head(h, False)
            diff_head(HEADS - 1, True)

            load_side(5, o_d[5])
            for k in range(4, KT):
                branch_a_hi(k)
                act.wait_ge(S["lo_done"], L_B1 + k + 1)
                load_side(k + 3, o_d[7] if k == 4 else gates_d[k + 3])

            def sigmoid_of(q):
                act.wait_ge(side_in[q % 3], 16 * (q // 3 + 1))
                act.activation(side(q), side(q), ACT.Sigmoid).then_inc(S["gate_sig"], 1)

            for m in range(3):
                sigmoid_of(Q_GA + m)
            for m in range(3, 8):
                act.wait_ge(S["acc_free"], A_B1 + m - 2)
                load_side(Q_GA + m, gates_d[8 + m])
                if m >= 4:
                    sigmoid_of(Q_GA + m - 1)
            def reused(k, used, done):
                if k < KT - 1:
                    act.wait_ge(S["a_used"], used + k + 1)
                else:
                    act.wait_ge(S["acc_done"], done)

            def load_branch_b(k):
                act.wait_ge(S["acc_free"], A_B1 + 6 + k)
                load_side(Q_B + k, o_d[8 + k])

            load_branch_b(0)
            sigmoid_of(Q_GA + 7)
            load_branch_b(1)
            for k in range(KT):
                if k == 2:
                    load_branch_b(2)
                reused(k, USED_B1, A_B2)
                act.wait_ge(side_in[(Q_B + k) % 3], 16 * ((Q_B + k) // 3 + 1))
                act.activation(ahi(k), side(Q_B + k), ACT.Copy).then_inc(S["hi_done"], 1)
                act.wait_ge(S["lo_done"], L_B2 + k + 1)
                load_side(Q_B + k + 3, o_d[8 + k + 3] if k < 5 else gates_d[16 + k - 5])
            for m in range(3):
                sigmoid_of(Q_GB + m)
            for m in range(3, 8):
                act.wait_ge(S["acc_free"], A_B2 + m - 2)
                load_side(Q_GB + m, gates_d[16 + m])
                if m >= 4:
                    sigmoid_of(Q_GB + m - 1)
            def load_residual(m):
                act.wait_ge(S["acc_free"], A_B2 + 6 + m)
                load_side(Q_X + m, xt_d[m])

            load_residual(0)
            sigmoid_of(Q_GB + 7)
            load_residual(1)
            for k in range(KT):
                if k == 7:
                    load_residual(2)
                reused(k, USED_B2, A_OUT)
                act.wait_ge(S["x_add"], k + 1)
                act.activation(ahi(k), x(k), ACT.Copy).then_inc(S["hi_done"], 1)
            for m in range(7):
                act.wait_ge(S["acc_free"], A_OUT + m + 1)
                if m >= 2:
                    act.wait_ge(S["ssq_done"], m - 1)
                act.activation(row(1) if m else row(0), x(m), ACT.Square).then_inc(S["sq_done"], 1)
                if m < 5:
                    load_side(Q_X + 3 + m, xt_d[3 + m])
            for c in range(3):
                if c < 2:
                    act.wait_ge(S["tail_x"], c + 1)
                else:
                    act.wait_ge(S["acc_free"], A_UP)
                act.wait_ge(S["ssq_done"], 6)
                act.activation(third_of(row(1), c), third_of(x(7), c), ACT.Square).then_inc(S["sq_done"], 1)
            roots_of_means(0, 0)
            hi_of_scaled(PRE_FFN)

            def conv_input(u, n, before, free):
                act.wait_ge(S["acc_done"], before)
                act.wait_ge(S["u_free"], free)
                src = acc(n)
                act.copy(u[:, GAP:GAP + 2 * THIRD].rearrange("p (c n) -> p c n", c=2), src[:, 0:2, :])
                act.copy(u[:, GAP + 2 * THIRD:GAP + NP], src[:, 2, 0:NP - 2 * THIRD])
                act.copy(u[:, 2 * GAP + NP:UW], src[:, 2, NP - 2 * THIRD:THIRD]).then_inc(S["acc_free"], 1)

            def silu_of(j):
                act.wait_ge(S["u_free"], j * 2 + 3)
                act.activation(row(1, CW), row(1, CW), ACT.Silu).then_inc(S["silu_done"], 1)

            def store_hidden(j):
                act.wait_ge(S["hid_done"], j + 2)
                out = hid_d[bass.ds(j, 1)].rearrange("k p n -> p (k n)")
                act.dma_start(out[:, 0:NP], row(5, NP)).then_inc(S["hid_st"], 16)
                act.dma_start(out[:, NP:NT], row(5, CW)[:, NP + GAP:CW]).then_inc(S["hid_st"], 16)

            def hi_of_hidden(g, third):
                act.wait_ge(hid_in[g], third * 16 + 16)
                for k in range(*hid_group(g)):
                    cut = slice(k * THIRD, (k + 1) * THIRD)
                    act.activation(a_hi[:, cut], a_pre[:, cut], ACT.Copy).then_inc(S["hi_done"], 1)

            with act.Fori(0, FT - 1) as j:
                conv_input(u_g, 0, j * 2 + (A_UP + 1), j * 2 + 1)
                conv_input(u_v, 1, j * 2 + (A_UP + 2), j * 2 + 2)
                silu_of(j)
                store_hidden(j)
            conv_input(u_g, 0, A_PLE - 1, FT * 2 - 1)
            silu_of(FT - 1)
            for g in range(2):
                hi_of_hidden(g, 0)
            conv_input(u_v, 1, A_PLE, FT * 2)
            store_hidden(FT - 1)
            for g in range(2, 4):
                hi_of_hidden(g, 0)
            act.wait_ge(S["hid_st"], 32 * (FT + 1))
            load_hidden(act, 4, 0)
            hi_of_hidden(4, 0)
            act.dma_start(ple_in[:, 0:LAST, :], t["p_prompt"][0, 0].rearrange("(i p) c -> p i c", p=P)).then_inc(S["ple_in"], 16)
            act.dma_start(ple_in[0:NS, LAST, :], t["p_sample"][0, 0]).then_inc(S["ple_in"], 16)

            def square_of_third(third, m):
                act.wait_ge(S["down_free"], third * 8 + (9 + m))
                cut = bass.ds(third * THIRD, THIRD)
                if m >= 2:
                    act.wait_ge(S["ssq_done"], third * 7 + (SSQ_DOWN + m - 1))
                act.activation(row(1, THIRD) if m else row(0)[:, cut], x(m)[:, cut],
                               ACT.Square).then_inc(S["sq_done"], 1)

            def weights_hi(third, m, following):
                for j in range(3 * m + 8, 3 * m + 11):
                    if j < 24 or following:
                        slot, words = (U_DOWN + j) % SLOTS, down_words(j)
                        act.wait_ge(S["down_done"], third * 8 + (m + 1))
                        act.wait_ge(w_landed[j % RAW], (third * 24 + (U_DOWN + j - j % RAW)) * 4 + 16)
                        act.activation(w_hi[:, slot, 0:words], w_raw[:, j % RAW, 0:words],
                                       ACT.Copy).then_inc(S["down_hi"], 1)

            def down_third(third, following):
                for m in range(7):
                    square_of_third(third, m)
                    weights_hi(third, m, following)
                if following:
                    for g in range(5):
                        if g < 4:
                            act.wait_ge(S["hid_used"], third * (FT - 1) + hid_group(g)[1])
                        else:
                            act.wait_ge(S["down_done"], third * 8 + 8)
                        load_hidden(act, g, third + 1)
                        if g:
                            hi_of_hidden(g - 1, third + 1)
                    hi_of_hidden(4, third + 1)
                    weights_hi(third, 7, following)
                square_of_third(third, 7)

            with act.Fori(0, 2) as third:
                down_third(third, True)
            down_third(2, False)
            def ple_hi_part(b):
                act.wait_ge(S["down_done"], 24)
                act.wait_ge(S["ple_tr"], b + 1)
                act.activation(ple_part(ple_hi, b), ple_block(b), ACT.Copy).then_inc(S["ple_hi"], 1)

            for b in range(5):
                ple_hi_part(b)
            roots_of_means(1, 3)
            hi_of_scaled(PRE_PLE)
            act.wait_ge(S["ul_ev"], 1)
            for w in range(4):
                out = t["conv_prompt" if w < 2 else "conv_sample"][0, 0, w % 2].rearrange("(b j c) -> j b c", b=2, c=P)
                act.dma_start(out, ul_rows[w:4 * FT:4, :].rearrange("p (b c) -> p b c", b=2)).then_inc(S["ul_st"], 16)
            for m in range(9):
                if m < 8:
                    act.wait_ge(S["acc_done"], A_PLE + (2 * m + 1 if m else 2))
                    if m:
                        act.wait_ge(S["y_mul"], m)
                    act.activation(thirds(row(0)), acc(1), ACT.Sigmoid).then_inc(S["sig_done"], 1)
                if m:
                    o, b = m - 1, (m - 1) % 2
                    if o >= 2:
                        act.wait_ge(y_st[b], 32 * (o // 2))
                    for part in range(3):
                        act.wait_ge(S["y_tr"], 3 * o + part + 1)
                        if part < 2:
                            act.copy(y_tok[:, b, 4 * part:4 * part + 4, :],
                                     ps[:, 6 + part, :].rearrange("p (i c) -> p i c", c=P)).then_inc(S["y_ev"], 1)
                        else:
                            act.copy(y_tok[0:NS, b, LAST, :], ps[0:NS, 6, 0:P]).then_inc(S["y_ev"], 1)
                    act.wait_ge(S["y_ev"], 3 * m)
                    act.dma_start(t["y_prompt"][0].rearrange("(i p) c -> p i c", p=P)[:, :, o * P:m * P],
                                  y_tok[:, b, 0:LAST, :]).then_inc(y_st[b], 16)
                    act.dma_start(t["y_sample"][0][:, o * P:m * P], y_tok[0:NS, b, LAST, :]).then_inc(y_st[b], 16)
            act.wait_ge(y_st[0], 32 * 4)
            act.wait_ge(y_st[1], 32 * 4)
            act.wait_ge(S["ul_st"], 64)

        @block.vector
        def _(dve):
            dve.memset(ones[:, :], 1.0)
            dve.memset(lamt[:, 8:9], 0.0).then_inc(S["down_free"], 8)
            dve.memset(eps[:, :], EPS).then_inc(S["lam_m"], 1)
            dve.wait_ge(S["gain_tr"], 1)
            dve.tensor_copy(cols[:, :], ps[:, 7, 0:26]).then_inc(S["gain_ev"], 1)
            dve.wait_ge(S["gain_ev"], 1)
            full_k = full[:, :].rearrange("p (k n) -> p k n", k=KT)
            for step in range(TILES + 3):
                i = step
                if i < TILES:
                    r, b = rows(i), i % 2
                    dve.wait_ge(S["xr_done"], i + 1)
                    dve.reciprocal(st[0:r, 4 + b:5 + b], st[0:r, 2 + b:3 + b]).then_inc(S["xi_done"], 1)
                    dve.wait_ge(S["xi_done"], i + 1)
                    dve.tensor_scalar(xn[0:r, b, :], xin[0:r, i % 3, :], st[0:r, 4 + b:5 + b], None,
                                      ALU.mult).then_inc(S["xn_done"], 1)
                    dve.wait_ge(S["x_tr"], i + 1)
                    dve.tensor_copy(full_k[:, 4:8, i * P:i * P + r],
                                    ps[:, 4, :].rearrange("p (k c) -> p k c", k=4)[:, :, 0:r]).then_inc(S["x_ev_d"], 1)
                i = step - 1
                if 0 <= i < TILES:
                    r = rows(i)
                    dve.wait_ge(S["xn_tr"], i + 1)
                    dve.tensor_tensor(a_pre_k[:, :, i * P:i * P + r],
                                      ps[:, 5:7, :].rearrange("p b (k c) -> p (b k) c", k=4)[:, :, 0:r],
                                      cols[:, 0:KT].unsqueeze(2).broadcast_to([P, KT, r]), ALU.mult).then_inc(S["pre_done"], 1)
                i = step - 3
                if 0 <= i < TILES:
                    r = rows(i)
                    at = slice(i * P, i * P + r)
                    dve.wait_ge(S["hi_done"], i + 1)
                    dve.tensor_tensor(a_lo_k[:, :, at], a_pre_k[:, :, at], a_hi_k[:, :, at].bitcast(F32),
                                      ALU.subtract).then_inc(S["lo_done"], 1)
            dve.wait_ge(S["vec_in"], 16 * 10)
            dve.tensor_tensor(lamt[:, 4:6], lamt[:, 0:2], lamt[:, 2:4], ALU.mult).then_inc(S["lam_m"], 1)
            dve.wait_ge(S["vec_tr"], 1)
            vp = ps[:, 7, :].rearrange("p (b c) -> p b c", b=4)
            dve.tensor_copy(convc[:, :, :].rearrange("p (b w) j -> p b (w j)", b=2), vp[:, 1:3, 0:4 * FT]).then_inc(S["vec_ev"], 1)
            dve.tensor_copy(convs[:, :, :].rearrange("p w j -> p (w j)"), vp[:, 3, 0:4 * FT]).then_inc(S["vec_ev"], 1)
            dve.tensor_scalar(cols[:, 24:26], cols[:, 24:26], 1.0 - LAM_INIT, None, ALU.mult).then_inc(S["vec_ev"], 1)
            dve.wait_ge(S["lam_e"], 1)
            dve.scalar_tensor_tensor(lam, lamt[:, 6:7], LAM_INIT, lamt[:, 7:8], ALU.add, ALU.subtract).then_inc(S["lam_d"], 1)

            def add_squares(v, w, squares, adds):
                dve.wait_ge(S["sq_done"], squares)
                if adds is not None:
                    dve.wait_ge(S["ssq_done"], adds)
                dve.tensor_tensor(v, v, w, ALU.add).then_inc(S["ssq_done"], 1)

            def lo_part(k, src, split0):
                dve.wait_ge(S["hi_done"], split0 + k + 1)
                dve.tensor_tensor(alo(k), src, ahi(k).bitcast(F32), ALU.subtract).then_inc(S["lo_done"], 1)

            def norm_and_split(norm, g, split0, norms):
                pieces = [(c, k) for c in range(3) for k in range(KT)]
                for n in range(len(pieces) + 2):
                    if n < len(pieces):
                        c, k = pieces[n]
                        inv = third_of(row(0), c)
                        if k == 0:
                            dve.wait_ge(S["rms_rt"], norms + c + 1)
                            dve.reciprocal(inv, inv).then_inc(S["rms_inv"], 1)
                            dve.wait_ge(S["rms_inv"], norms + c + 1)
                        dve.scalar_tensor_tensor(third_of(apre(k), c), third_of(x(k), c),
                                                 cols[:, g + k:g + k + 1], inv, ALU.mult, ALU.mult).then_inc(S["pre_done"], 1)
                    if n >= 2 and not on_pool(norm, n - 2):
                        c, k = pieces[n - 2]
                        dve.wait_ge(S["hi_done"], split0 + n - 1)
                        dve.tensor_tensor(third_of(alo(k), c), third_of(apre(k), c), third_of(ahi(k), c).bitcast(F32),
                                          ALU.subtract).then_inc(S["lo_done"], 1)

            dve.wait_ge(S["head_const"], 5 * 16)
            dve.tensor_scalar(gqk[:, 0, :], gqk[:, 0, :], DK ** -0.5, None, ALU.mult).then_inc(S["g_scaled"], 1)

            def rotate(src, i, groups, prods, before_p, done, in_place):
                r, ti = rows(i), i if i < LAST else PAST // P
                a = nrm[0:r, 0:groups * P].rearrange("p (g s c) -> p g s c", g=groups, s=2)
                bb = rope_b[0:r, 0:groups * P].rearrange("p (g s c) -> p g s c", g=groups, s=2)
                x4 = src.rearrange("p (g s c) -> p g s c", g=groups, s=2)
                sn = bcast(sin[0:r, ti, :], groups)
                dve.tensor_tensor(bb[:, :, 0, :], x4[:, :, 1, :], sn, ALU.mult).then_inc(prods, 1)
                dve.tensor_tensor(bb[:, :, 1, :], x4[:, :, 0, :], sn, ALU.mult).then_inc(prods, 1)
                if in_place:
                    dve.wait_ge(prods, before_p + 2)
                dve.tensor_tensor(a.rearrange("p g s c -> p (g s) c"), src.rearrange("p (g c) -> p g c", c=DK // 2),
                                  bcast(cos[0:r, ti, :], 2 * groups), ALU.mult).then_inc(prods, 1)
                dve.wait_ge(prods, before_p + 3)
                out = qk[0:r, i % 2, 0:groups * P].rearrange("p (g s c) -> p g s c", g=groups, s=2)
                dve.tensor_tensor(out[:, :, 0, :], a[:, :, 0, :], bb[:, :, 0, :], ALU.subtract).then_inc(done, 1)
                dve.tensor_tensor(out[:, :, 1, :], a[:, :, 1, :], bb[:, :, 1, :], ALU.add).then_inc(done, 1)

            with dve.Fori(0, HEADS) as h:
                c9 = h * TILES
                dve.wait_ge(S["head_in"], h * 64 + 64)
                for step in range(TILES + 4):
                    c = step - TILES - 1
                    if 0 <= c < 3:
                        if c < 2:
                            dve.wait_ge(S["gate_part"], h * 2 + (c + 1))
                        else:
                            dve.wait_ge(S["acc_done"], h + (FIRST + 1))
                        if c == 0:
                            dve.wait_ge(gate_st[0], h * 16 + FIRST // 2 * 16)
                        dve.tensor_copy(third_of(gate_row, c), ps[:, c, 0:THIRD]).then_inc(S["acc_free" if c == 2 else "gate_ev"], 1)
                    i = step
                    if i < TILES:
                        r = rows(i)
                        dve.wait_ge(S["v_done"], c9 + (i + 1))
                        if i >= 1:
                            dve.wait_ge(S["rope_done"], h * (2 * TILES) + 2 * i)
                        if i >= 2:
                            dve.wait_ge(S["qk_tr"], c9 + (i - 1))
                            dve.wait_ge(S["kd_done"], c9 + (i - 1))
                        rotate(ps[0:r, i % 3, 0:2 * P], i, 2, S["rope_m"], h * (3 * TILES) + 3 * i,
                               S["rope_done"], False)
                        dve.wait_ge(S["rope_done"], h * (2 * TILES) + 2 * (i + 1))
                        if i >= 3:
                            dve.wait_ge(S["kv_done"], c9 + (i - 2))
                        c = 2 * P + (i == LAST)
                        dve.tensor_scalar(kd[0:r, i % 3, :], qk[0:r, i % 2, P:2 * P], hc[0:r, c:c + 1], None,
                                          ALU.mult).then_inc(S["kd_done"], 1)
                    i = step - 1
                    if 0 <= i < TILES:
                        r = rows(i)
                        dve.wait_ge(S["qk_ev"], c9 + (i + 1))
                        if i >= 2:
                            dve.wait_ge(S["o_done"], c9 + (i - 1))
                        dve.tensor_tensor(q_d[:, i % 2, 0:r], qk_t[:, i % 2, 0:r], hc[:, P:P + r],
                                          ALU.mult).then_inc(S["qd_done"], 1)
                    i = step - 2
                    if 0 <= i < TILES:
                        r = rows(i)
                        dve.wait_ge(S["sc_done"], c9 + (i + 1))
                        dve.tensor_tensor(s_m[0:r, i % 2, 0:r], ps[0:r, 5, 0:r], hc[0:r, 0:r],
                                          ALU.mult).then_inc(S["sm_done"], 1)
                    i = step - 3
                    if 0 <= i < TILES:
                        r, b = rows(i), i % 2
                        dve.wait_ge(S["kv_done"], c9 + (i + 1))
                        if i == 0:
                            dve.tensor_copy(s_p, ps[:, 7, 0:DV]).then_inc(S["state_done"], 1)
                        else:
                            s_x, c = (s_p, 2 * P + 2) if i < LAST else (s_s, 2 * P + 3)
                            dve.wait_ge(S["state_done"], c9 + i)
                            dve.scalar_tensor_tensor(s_x, s_x, hc[:, c:c + 1], ps[:, 7, 0:DV],
                                                     ALU.mult, ALU.add).then_inc(S["state_done"], 1)
                        dve.wait_ge(S["o_rt"], c9 + (i + 1))
                        dve.reciprocal(st[0:r, 4 + b:5 + b], st[0:r, 2 + b:3 + b]).then_inc(S["o_inv"], 1)
                    i = step - 4
                    if 0 <= i < TILES:
                        r, b = rows(i), i % 2
                        dve.wait_ge(S["ot_tr"], c9 + (i + 1))
                        if i >= 2:
                            dve.wait_ge(ot_st[b], h * (16 * (5 - b)) + 16 * (i // 2))
                        for m in range(2):
                            last = dve.tensor_tensor(o_t[:, b, m, 0:r], ps[:, 3, m * P:m * P + r],
                                                     gates_h[m][:, i * P:i * P + r], ALU.mult)
                        last.then_inc(S["ot_ev"], 1)
                dve.wait_ge(S["ot_ev"], c9 + TILES)

            dve.wait_ge(S["g_scaled"], 1)
            dve.wait_ge(S["lam_d"], 1)
            with dve.Fori(0, HEADS) as h:
                c9 = h * TILES
                for step in range(DIFF_STEPS):
                    for n in (2 * (step - TILES - 1), 2 * (step - TILES - 1) + 1):
                        if 0 <= n < 6:
                            wait_piece(dve, h, n, S["acc_done"], S["gate_part"])
                            if n == 0:
                                dve.wait_ge(S["d_rope"], h * (2 * TILES) + 2 * TILES)
                            if n >= 2:
                                dve.wait_ge(part_st[n % 2], h * 48 + 16 * (n // 2))
                            dve.tensor_copy(gate_piece(n), ps[:, (3 + n) % 4, 0:THIRD]).then_inc(S["acc_free" if n % 3 == 2 else "gate_ev"], 1)
                    if step == TILES:
                        dve.wait_ge(S["dc_tr"], h + 1)
                        dve.tensor_copy(k_t[:, :, NT:NT + PAST],
                                        ps[:, 2, 0:2 * P].rearrange("p (m n) -> p m n", m=2)).then_inc(S["dc_ev"], 1)
                    i = step - 4
                    if 0 <= i < TILES:
                        r, b = rows(i), i % 2
                        dve.wait_ge(S["do_rt"], c9 + (i + 1))
                        dve.reciprocal(st[0:r, 4 + b:5 + b], st[0:r, 2 + b:3 + b]).then_inc(S["do_inv"], 1)
                    i = step - 2
                    if 0 <= i < TILES:
                        r, b = rows(i), i % 2
                        keys = P * (i + 1) if i < LAST else NS + PAST
                        dve.wait_ge(S["s0_done"], c9 + (i + 1))
                        dve.tensor_reduce(st[0:r, 24 + b:25 + b], s_bank[0:r, 0:keys], axis=AX_X, op=ALU.max,
                                          negate=True).then_inc(S["m0_done"], 1)
                    i = step - 3
                    if 0 <= i < TILES:
                        r, n = rows(i), min(4, i + 1) if i < LAST else 2
                        dve.wait_ge(S["at0_tr"], c9 + (i + 1))
                        if i >= 1:
                            dve.wait_ge(S["pv_done"], c9 + i)
                        dve.tensor_copy(a_t[:, 0:n, 0:r],
                                        ps[:, 4, :].rearrange("p (b n) -> p b n", b=4)[:, 0:n, 0:r]).then_inc(S["at0_ev"], 1)
                    i = step - 1
                    if 0 <= i < TILES:
                        r, b = rows(i), i % 2
                        dve.wait_ge(S["d_rt"], c9 + (i + 1))
                        dve.reciprocal(st[0:r, 36 + 4 * b:40 + 4 * b], st[0:r, 16 + 4 * b:20 + 4 * b]).then_inc(S["d_inv"], 1)
                        dve.wait_ge(S["d_inv"], c9 + (i + 1))
                        for m in range(4):
                            bank, at = (2 * b, m * P) if m < 3 else (2 * b + 1, 0)
                            if m == 3:
                                dve.wait_ge(S["d_v"], c9 + (i + 1))
                            dve.scalar_tensor_tensor(nrm[0:r, m * P:(m + 1) * P], ps[0:r, bank, at:at + P],
                                                     st[0:r, 36 + 4 * b + m:37 + 4 * b + m], gqk[0:r, m // 2, :],
                                                     ALU.mult, ALU.mult).then_inc(S["d_nrm"], 1)
                        dve.wait_ge(S["d_nrm"], h * (4 * TILES) + 4 * (i + 1))
                        if i >= 2:
                            dve.wait_ge(S["d_tr"], c9 + (i - 1))
                            dve.wait_ge(k_st[b], h * (16 * (5 - b)) + 16 * (i // 2))
                        rotate(nrm[0:r, :], i, 4, S["d_ropem"], h * (3 * TILES) + 3 * i, S["d_rope"], True)
                    i = step - 2
                    if 0 <= i < TILES:
                        r, b = rows(i), i % 2
                        dve.wait_ge(S["s1_done"], c9 + (i + 1))
                        dve.tensor_reduce(st[0:r, 26 + b:27 + b], s_bank[0:r, 0:keys], axis=AX_X, op=ALU.max,
                                          negate=True).then_inc(S["m1_done"], 1)
                    i = step - 3
                    if 4 <= i < LAST:
                        dve.wait_ge(S["at1_tr"], h * 4 + (i - 3))
                        dve.tensor_copy(a_t[:, 4:i + 1, :],
                                        ps[:, 4, 0:(i - 3) * P].rearrange("p (b n) -> p b n", n=P)).then_inc(S["at1_ev"], 1)
                    i = step - 2
                    if 0 <= i < TILES:
                        r, b = rows(i), i % 2
                        dve.wait_ge(S["e1_done"], c9 + (i + 1))
                        dve.reciprocal(st[0:r, 32 + 2 * b:34 + 2 * b], st[0:r, 28 + 2 * b:30 + 2 * b]).then_inc(S["r_inv"], 1)
                        dve.wait_ge(S["r_inv"], c9 + (i + 1))
                        r1 = st[0:r, 33 + 2 * b:34 + 2 * b]
                        dve.tensor_tensor(r1, r1, lam[0:r, :], ALU.mult).then_inc(S["r_lam"], 1)
                        dve.wait_ge(S["r_lam"], c9 + (i + 1))
                        dve.tensor_scalar(e1[0:r, 0:keys], e1[0:r, 0:keys], r1, None, ALU.mult).then_inc(S["t_done"], 1)
                        dve.wait_ge(S["t_done"], c9 + (i + 1))
                        if i >= 1:
                            dve.wait_ge(S["at0_tr"], c9 + i)
                        if 4 <= i - 1 < LAST:
                            dve.wait_ge(S["at1_tr"], h * 4 + (i - 4))
                        dve.scalar_tensor_tensor(a_w[0:r, 0:keys], e0[0:r, 0:keys], st[0:r, 32 + 2 * b:33 + 2 * b],
                                                 e1[0:r, 0:keys], ALU.mult, ALU.subtract).then_inc(S["a_done"], 1)
                    i = step - 1
                    if 0 <= i < TILES:
                        r, b = rows(i), i % 2
                        dve.wait_ge(S["d_tr"], c9 + (i + 1))
                        if i >= 2:
                            dve.wait_ge(S["s1_done"], c9 + (i - 1))
                        v4 = ps[:, 4, :].rearrange("p (m n) -> p m n", m=4)
                        dve.tensor_copy(q_t[:, b, :, 0:r], v4[:, 0:2, 0:r]).then_inc(S["d_ev"], 1)
                        dve.tensor_copy(k_t[:, :, i * P:i * P + r], v4[:, 2:4, 0:r]).then_inc(S["d_ev"], 1)
                dve.wait_ge(S["dot_ev"], h * (2 * TILES) + 2 * TILES)
                dve.wait_ge(part_st[0], h * 48 + 48)
                dve.wait_ge(part_st[1], h * 48 + 48)

            for k in range(KT):
                lo_part(k, side(Q_A + k), L_B1)
            for m in range(8):
                if m == 7:
                    for k in range(2):
                        lo_part(k, side(Q_B + k), L_B2)
                q = Q_GA + m
                dve.wait_ge(S["gate_sig"], m + 1)
                dve.wait_ge(S["acc_done"], A_B1 + m + 1)
                dve.tensor_tensor(thirds(x(m)), acc(m), thirds(side(q)), ALU.mult).then_inc(S["acc_free"], 1)
            for k in range(2, KT):
                lo_part(k, side(Q_B + k), L_B2)
            for m in range(8):
                if m == 7:
                    for k in range(7):
                        if k == 0:
                            dve.wait_ge(S["x_add"], 7)
                        lo_part(k, x(k), L_OUT)
                q = Q_GB + m
                dve.wait_ge(S["gate_sig"], 8 + m + 1)
                dve.wait_ge(S["acc_done"], A_B2 + m + 1)
                if m >= 2:
                    dve.wait_ge(S["x_add"], m - 1)
                else:
                    dve.wait_ge(S["lo_done"], L_B1 + KT)
                dve.tensor_tensor(thirds(row(1 + m % 2)), acc(m), thirds(side(q)), ALU.mult).then_inc(S["acc_free"], 1)
                dve.wait_ge(S["acc_free"], A_B2 + m + 1)
                dve.tensor_tensor(x(m), x(m), row(1 + m % 2), ALU.add).then_inc(S["x_add"], 1)
            dve.wait_ge(S["x_add"], 8)
            lo_part(7, x(7), L_OUT)
            dve.wait_ge(S["lo_done"], L_OUT + KT)
            for m in range(9):
                if m < 8:
                    q = Q_X + m
                    dve.wait_ge(side_in[q % 3], 16 * (q // 3 + 1))
                    dve.wait_ge(S["acc_done"], A_OUT + m + 1)
                if m < 7:
                    dve.tensor_tensor(thirds(x(m)), acc(m), thirds(side(q)), ALU.add).then_inc(S["acc_free"], 1)
                elif m == 7:
                    for c in range(3):
                        last = dve.tensor_tensor(third_of(x(7), c), acc(7)[:, c, :], third_of(side(q), c), ALU.add)
                        last.then_inc(S["tail_x" if c < 2 else "acc_free"], 1)
                if 2 <= m < 8:
                    add_squares(row(0), row(1), m, m - 2 if m > 2 else None)
            for c in range(3):
                add_squares(third_of(row(0), c), third_of(row(1), c), 8 + c, 6)
            norm_and_split(0, 8, L_FFN, 0)

            dve.wait_ge(S["acc_free"], A_UP)
            dve.wait_ge(S["lo_done"], L_DOWN)
            dve.memset(u_g[:, 0:GAP], 0.0).then_inc(S["u_free"], 1)
            dve.memset(u_v[:, 0:GAP], 0.0).then_inc(S["u_free"], 1)
            dve.memset(row(5, 2), 0.0).then_inc(S["hid_done"], 1)
            dve.wait_ge(S["hid_done"], 1)
            dve.memset(row(5, 2), 0.0).then_inc(S["hid_st"], 32)
            def conv(j, half):
                u, c = ((u_g, row(1, CW)), (u_v, row(2, CW)))[half]

                def col(w):
                    return convc[:, w, bass.ds(j + half * FT, 1)]

                dve.wait_ge(S["u_free"], j * 2 + (half + 1))
                dve.tensor_copy(u[:, GAP + NP:2 * GAP + NP], convs[:, :, bass.ds(j + half * FT, 1)].rearrange("p w a -> p (w a)")).then_inc(S["u_pad"], 1)
                dve.wait_ge(S["acc_free"], j * 2 + (A_UP + half + 1))
                at = (3 + half) * UW + NP
                ends = scr[:, at:at + 2 * (NS + GAP)].rearrange("p (a b) -> p a b", a=2)[:, :, 0:GAP]
                dve.tensor_copy(u_last[:, bass.ds(j + half * FT, 1), :].rearrange("p a (s w) -> p (a s) w", w=GAP),
                                ends).then_inc(S["u_last_done"], 1)
                dve.wait_ge(S["u_pad"], j * 2 + (half + 1))
                dve.wait_ge(S["hid_done"], j + 1)
                dve.tensor_scalar(c, u[:, 2:2 + CW], col(2), col(3), ALU.mult, ALU.add).then_inc(S["conv_t"], 1)
                dve.wait_ge(S["conv_t"], j * 4 + (2 * half + 1))
                dve.scalar_tensor_tensor(c, u[:, 1:1 + CW], col(1), c, ALU.mult, ALU.add).then_inc(S["conv_t"], 1)
                dve.wait_ge(S["conv_t"], j * 4 + (2 * half + 2))
                dve.scalar_tensor_tensor(c, u[:, 0:CW], col(0), c, ALU.mult, ALU.add).then_inc(S["u_free"], 1)

            def hidden(j):
                dve.wait_ge(S["silu_done"], j + 1)
                dve.wait_ge(S["u_free"], j * 2 + 4)
                dve.wait_ge(S["hid_st"], j * 32 + 32)
                dve.tensor_tensor(row(5, CW), row(1, CW), row(2, CW), ALU.mult).then_inc(S["hid_done"], 1)

            def lo_of_hidden(g, third):
                for k in range(*hid_group(g)):
                    cut = slice(k * THIRD, (k + 1) * THIRD)
                    dve.wait_ge(S["hi_done"], third * FT + (H_DOWN + k + 1))
                    dve.tensor_tensor(a_lo[:, cut], a_pre[:, cut], a_hi[:, cut].bitcast(F32),
                                      ALU.subtract).then_inc(S["lo_done"], 1)

            with dve.Fori(0, FT - 1) as j:
                conv(j, 0)
                conv(j, 1)
                hidden(j)
            conv(FT - 1, 0)
            for g in range(2):
                lo_of_hidden(g, 0)
            conv(FT - 1, 1)
            hidden(FT - 1)
            for g in range(2, 5):
                lo_of_hidden(g, 0)

            def down_sum(third, m):
                cut = bass.ds(third * THIRD, THIRD)
                dve.wait_ge(S["down_done"], third * 8 + (m + 1))
                dve.tensor_tensor(x(m)[:, cut], x(m)[:, cut], ps[:, (m + 6) % 8, 0:THIRD], ALU.add).then_inc(S["down_free"], 1)

            def down_squares(third, m):
                add_squares(row(0)[:, bass.ds(third * THIRD, THIRD)], row(1, THIRD),
                            third * 8 + (10 + m + 1), third * 7 + (SSQ_DOWN + m - 1))

            def down_third(third, following):
                for m in range(7):
                    down_sum(third, m)
                    if m >= 2:
                        down_squares(third, m - 1)
                down_squares(third, 6)
                if following:
                    for g in range(5):
                        lo_of_hidden(g, third + 1)
                down_sum(third, 7)
                down_squares(third, 7)

            def ple_lo_part(b):
                dve.wait_ge(S["ple_hi"], b + 1)
                dve.tensor_tensor(ple_part(ple_lo, b), ple_block(b), ple_part(ple_hi, b).bitcast(F32),
                                  ALU.subtract).then_inc(S["ple_lo"], 1)

            with dve.Fori(0, 2) as third:
                down_third(third, True)
            down_third(2, False)
            dve.wait_ge(S["ul_tr"], 1)
            dve.tensor_copy(ul_rows[0:4 * FT, :], ps[0:4 * FT, 0, 0:2 * P]).then_inc(S["ul_ev"], 1)
            for b in range(2):
                ple_lo_part(b)
            for b in range(2, 5):
                ple_lo_part(b)
            norm_and_split(1, 16, H_PLE, 3)
            for m in range(8):
                dve.wait_ge(S["sig_done"], m + 1)
                dve.wait_ge(S["acc_done"], A_PLE + 2 * m + 2)
                if m:
                    dve.wait_ge(S["y_done"], m)
                dve.tensor_tensor(thirds(row(1)), acc(0), thirds(row(0)), ALU.mult).then_inc(S["y_mul"], 1)
                dve.wait_ge(S["y_mul"], m + 1)
                dve.tensor_tensor(x(m), x(m), row(1), ALU.add).then_inc(S["y_done"], 1)


INPUTS = ["x_prompt", "x_sample", "cache_k", "cache_v", "state_ret", "state_conv", "p_prompt", "p_sample",
          "g_mix", "w_in", "g_qn", "g_kn", "lam_q1", "lam_k1", "lam_q2", "lam_k2", "g_dnorm", "w_ret_br",
          "w_da_br", "w_out", "g_ffn", "w_up", "conv_w", "conv_b", "w_down", "g_ple", "w_ple_gate", "w_ple"]
OUTPUTS = [("y_prompt", (1, NP, D)), ("y_sample", (1, NS, D)),
           ("new_k_prompt", (1, 1, NP, HEADS, 2, DK)), ("new_k_sample", (1, 1, NS, HEADS, 2, DK)),
           ("new_v_prompt", (1, 1, NP, HEADS, DV)), ("new_v_sample", (1, 1, NS, HEADS, DV)),
           ("ret_prompt", (1, 1, HEADS, DK, DV)), ("ret_sample", (1, 1, HEADS, DK, DV)),
           ("conv_prompt", (1, 1, 2, 2 * FF)), ("conv_sample", (1, 1, 2, 2 * FF))]


def shape_constants():
    import numpy as np
    inv = np.float32(10000.0) ** (-np.arange(0, DK, 2, dtype=np.float32) / np.float32(DK))
    ang = np.arange(NP, dtype=np.float32)[:, None] * inv[None, :].astype(np.float32)
    ang = ang.reshape(NP // P, P, DK // 2).transpose(1, 0, 2)
    idx = np.arange(P, dtype=np.float64)
    ret = np.zeros((HEADS, P, HC))
    for h in range(HEADS):
        log_g = np.log(1.0 - 2.0 ** (-5.0 - h))
        diff = idx[None, :] - idx[:, None]
        ret[h, :, 0:P] = np.where(diff >= 0, np.exp(log_g * np.maximum(diff, 0)), 0.0) * DK ** -0.5
        ret[h, :, P:2 * P] = np.exp((idx + 1) * log_g)[None, :]
        ret[h, :, 2 * P] = np.exp((P - 1 - idx) * log_g) * DK ** -0.5
        ret[h, :, 2 * P + 1] = np.exp((NS - 1 - idx) * log_g) * DK ** -0.5
        ret[h, :, 2 * P + 2] = np.exp(P * log_g)
        ret[h, :, 2 * P + 3] = np.exp(NS * log_g)
    mask = np.zeros((1, 2 * P))
    mask[0, 0:P // 2] = 1.0
    mask[0, P + P // 2:] = MASKED
    out = {"c_cos": np.cos(ang), "c_sin": np.sin(ang), "c_ret": ret, "c_mask": mask, "c_ident": np.eye(P)}
    return {k: np.ascontiguousarray(v.astype(np.float32)) for k, v in out.items()}


def kernel(**inputs):
    import numpy as np
    import concourse.bacc as bacc
    from concourse.bass_utils import run_bass_kernel_spmd

    nc = bacc.Bacc("TRN2", target_bir_lowering=False, num_devices=1)
    arrays = {n: np.ascontiguousarray(inputs[n]) for n in INPUTS}
    arrays.update(shape_constants())
    t = {n: nc.dram_tensor(n, a.shape, F32, kind="ExternalInput").ap() for n, a in arrays.items()}
    for n, shape in OUTPUTS:
        t[n] = nc.dram_tensor(n, shape, F32, kind="ExternalOutput").ap()
    kernel_program(nc, t)
    r = run_bass_kernel_spmd(nc, [arrays], core_ids=[0])
    return tuple(r.results[0][n] for n, _ in OUTPUTS)
```
